# Optimizing a Trainium2 kernel written in Bass

```python
import jax, jax.numpy as jnp
from jax import lax
import numpy as np

D_MODEL = 1024
BATCH = 1
SEQ = 512
DEPTH = 2

GRID_W = 64
CTX_LEN = 256
N_Q_HEADS = 8
N_KV_HEADS = 2
HEAD_DIM = 64
ATTN_WIDTH = N_Q_HEADS * HEAD_DIM
KV_WIDTH = N_KV_HEADS * HEAD_DIM
Q_BLOCK = 128
ROPE_THETA = 10000.0
POOL_WINDOWS = (2, 4, 8, 16)
N_POOL_GROUPS = 4
POOL_GROUP_DIM = 128
POOL_WIDTH = N_POOL_GROUPS * POOL_GROUP_DIM
MIX_IN_WIDTH = ATTN_WIDTH + 2 * KV_WIDTH + POOL_WIDTH
MIX_OUT_WIDTH = ATTN_WIDTH + POOL_WIDTH
CONV_WIDTH = D_MODEL
CONV_K = 3
N_EXPERTS = 16
EXPERT_FF = 1024
CAPACITY_FACTOR = 2
NORM_EPS = 1e-6
DEEPNORM_ALPHA = (2 * DEPTH) ** 0.25
DEEPNORM_BETA = (8 * DEPTH) ** -0.25


def _layer_norm(x, g, b):
    xf = x.astype(jnp.float32)
    mu = jnp.mean(xf, axis=-1, keepdims=True)
    xc = xf - mu
    var = jnp.mean(xc * xc, axis=-1, keepdims=True)
    y = xc * lax.rsqrt(var + NORM_EPS) * g.astype(jnp.float32) + b.astype(jnp.float32)
    return y.astype(x.dtype)

def _rms_norm(x, g):
    xf = x.astype(jnp.float32)
    y = xf * lax.rsqrt(jnp.mean(xf * xf, axis=-1, keepdims=True) + NORM_EPS)
    return (y * g.astype(jnp.float32)).astype(x.dtype)

def _modulation(cond, w, b):
    m = (cond @ w + b)[:, None, :]
    return jnp.split(m, 6, axis=-1)

def _modulate(h, shift, scale):
    return h * (1.0 + scale) + shift

def _post_norm(h, branch, g, b):
    return _layer_norm(DEEPNORM_ALPHA * h + branch, g, b)

def _axial_rope_tables(rows):
    row = jnp.broadcast_to(jnp.arange(rows, dtype=jnp.float32)[:, None], (rows, GRID_W)).reshape(-1)
    col = jnp.broadcast_to(jnp.arange(GRID_W, dtype=jnp.float32)[None, :], (rows, GRID_W)).reshape(-1)
    axis_dim = HEAD_DIM // 2
    inv_freq = ROPE_THETA ** (-jnp.arange(0, axis_dim, 2, dtype=jnp.float32) / axis_dim)
    ang = jnp.concatenate([row[:, None] * inv_freq, col[:, None] * inv_freq], axis=-1)
    return jnp.cos(ang), jnp.sin(ang)

def _apply_rope(x, cos, sin):
    xf = x.astype(jnp.float32).reshape(x.shape[:-1] + (HEAD_DIM // 2, 2))
    x0, x1 = xf[..., 0], xf[..., 1]
    c = cos[None, :, None, :]
    s = sin[None, :, None, :]
    out = jnp.stack([x0 * c - x1 * s, x0 * s + x1 * c], axis=-1).reshape(x.shape)
    return out.astype(x.dtype)

def _blocked_attention(q, k, v):
    b, lq = q.shape[:2]
    grp = N_Q_HEADS // N_KV_HEADS
    nb = lq // Q_BLOCK
    qb = q.reshape(b, nb, Q_BLOCK, N_KV_HEADS, grp, HEAD_DIM).transpose(1, 0, 2, 3, 4, 5)
    scale = HEAD_DIM ** -0.5

    def one_block(qi):
        s = jnp.einsum('bqhgd,bkhd->bhgqk', qi, k, preferred_element_type=jnp.float32) * scale
        p = jax.nn.softmax(s, axis=-1)
        return jnp.einsum('bhgqk,bkhd->bqhgd', p.astype(v.dtype), v)

    o = lax.map(one_block, qb)
    return o.transpose(1, 0, 2, 3, 4, 5).reshape(b, lq, ATTN_WIDTH)

def _pool_branch(p, w_grp, p_scale):
    b, l, _ = p.shape
    pf = p.astype(jnp.float32)
    cs = jnp.concatenate([jnp.zeros((b, 1, POOL_WIDTH), jnp.float32), jnp.cumsum(pf, axis=1)], axis=1)
    t = jnp.arange(l)
    means = []
    for g, w in enumerate(POOL_WINDOWS):
        lo = jnp.maximum(t - w // 2, 0)
        hi = jnp.minimum(t + w // 2, l)
        seg = cs[:, :, g * POOL_GROUP_DIM:(g + 1) * POOL_GROUP_DIM]
        cnt = (hi - lo).astype(jnp.float32)[None, :, None]
        means.append((seg[:, hi] - seg[:, lo]) / cnt)
    pooled = (jnp.concatenate(means, axis=-1) - pf).astype(p.dtype)
    pooled = pooled.reshape(b, l, N_POOL_GROUPS, POOL_GROUP_DIM)
    out = jnp.einsum('blgc,gcd->blgd', pooled, w_grp).reshape(b, l, POOL_WIDTH)
    return out * p_scale

def _split_mix_in(h):
    return jnp.split(h, [ATTN_WIDTH, ATTN_WIDTH + KV_WIDTH, ATTN_WIDTH + 2 * KV_WIDTH], axis=-1)

def _attn_pool_mixer(u_lat, u_ctx, cos, sin, w_in, q_g, k_g, w_grp, p_scale, w_out, ctx_out):
    b, s, _ = u_lat.shape
    lc = u_ctx.shape[1]
    q, k, v, p = _split_mix_in(u_lat @ w_in)
    q = _apply_rope(_rms_norm(q.reshape(b, s, N_Q_HEADS, HEAD_DIM), q_g), cos, sin)
    k = _apply_rope(_rms_norm(k.reshape(b, s, N_KV_HEADS, HEAD_DIM), k_g), cos, sin)
    v = v.reshape(b, s, N_KV_HEADS, HEAD_DIM)
    if ctx_out:
        qc, kc, vc, pc = _split_mix_in(u_ctx @ w_in)
    else:
        kc, vc = jnp.split(u_ctx @ w_in[:, ATTN_WIDTH:ATTN_WIDTH + 2 * KV_WIDTH], 2, axis=-1)
    kc = _rms_norm(kc.reshape(b, lc, N_KV_HEADS, HEAD_DIM), k_g)
    vc = vc.reshape(b, lc, N_KV_HEADS, HEAD_DIM)
    k_all = jnp.concatenate([kc, k], axis=1)
    v_all = jnp.concatenate([vc, v], axis=1)
    a_lat = _blocked_attention(q, k_all, v_all)
    y_lat = jnp.concatenate([a_lat, _pool_branch(p, w_grp, p_scale)], axis=-1) @ w_out
    y_ctx = None
    if ctx_out:
        qc = _rms_norm(qc.reshape(b, lc, N_Q_HEADS, HEAD_DIM), q_g)
        a_ctx = _blocked_attention(qc, kc, vc)
        y_ctx = jnp.concatenate([a_ctx, _pool_branch(pc, w_grp, p_scale)], axis=-1) @ w_out
    return y_lat, y_ctx

def _short_conv_mixer(u, w_in, conv_w, w_out):
    b_gate, c_gate, x_in = jnp.split(u @ w_in, 3, axis=-1)
    z = lax.conv_general_dilated(c_gate * x_in, conv_w[:, None, :], window_strides=(1,),
                                 padding=((CONV_K // 2, CONV_K // 2),),
                                 dimension_numbers=('NWC', 'WIO', 'NWC'),
                                 feature_group_count=CONV_WIDTH)
    return (b_gate * z) @ w_out

def _expert_choice_ffn(u, w_router, w_g, w_u, w_d):
    b, n, _ = u.shape
    cap = CAPACITY_FACTOR * n // N_EXPERTS
    logits = jnp.einsum('bnd,de->ben', u, w_router, preferred_element_type=jnp.float32)
    aff = jax.nn.softmax(logits, axis=1)
    gate, idx = lax.top_k(aff, cap)
    bidx = jnp.arange(b)[:, None, None]
    xe = u[bidx, idx]
    hg = jnp.einsum('becd,edf->becf', xe, w_g)
    hu = jnp.einsum('becd,edf->becf', xe, w_u)
    ye = jnp.einsum('becf,efd->becd', jax.nn.silu(hg) * hu, w_d) * gate[..., None].astype(u.dtype)
    return jnp.zeros_like(u).at[bidx, idx].add(ye)

def first_inputs(seed: int = 0) -> dict:
    key = jax.random.key(seed)
    ks = jax.random.split(key, 24)
    f32 = jnp.float32
    n_even = (DEPTH + 1) // 2
    n_odd = DEPTH // 2

    def dense(k, shape, fan_in, mult=1.0):
        return jax.random.normal(k, shape, f32) * (mult * fan_in ** -0.5)

    def gain(k, shape):
        return 1.0 + 0.02 * jax.random.normal(k, shape, f32)

    def small(k, shape):
        return 0.02 * jax.random.normal(k, shape, f32)

    return {
        'x': jax.random.normal(ks[0], (BATCH, SEQ, D_MODEL), f32),
        'c': jax.random.normal(ks[1], (BATCH, D_MODEL), f32),
        'ctx': jax.random.normal(ks[2], (BATCH, CTX_LEN, D_MODEL), f32),
        'c_ctx': jax.random.normal(ks[3], (D_MODEL,), f32),
        'w_mod': dense(ks[4], (DEPTH, D_MODEL, 6 * D_MODEL), D_MODEL, 0.5),
        'b_mod': 0.01 * jax.random.normal(ks[5], (DEPTH, 6 * D_MODEL), f32),
        'ln_mix_g': gain(ks[6], (DEPTH, D_MODEL)),
        'ln_mix_b': small(ks[7], (DEPTH, D_MODEL)),
        'ln_ffn_g': gain(ks[8], (DEPTH, D_MODEL)),
        'ln_ffn_b': small(ks[9], (DEPTH, D_MODEL)),
        'w_mix_in': dense(ks[10], (n_even, D_MODEL, MIX_IN_WIDTH), D_MODEL),
        'q_norm_g': gain(ks[11], (n_even, HEAD_DIM)),
        'k_norm_g': gain(ks[12], (n_even, HEAD_DIM)),
        'w_pool_grp': dense(ks[13], (n_even, N_POOL_GROUPS, POOL_GROUP_DIM, POOL_GROUP_DIM), POOL_GROUP_DIM),
        'pool_scale': gain(ks[14], (n_even, POOL_WIDTH)),
        'w_mix_out': dense(ks[15], (n_even, MIX_OUT_WIDTH, D_MODEL), MIX_OUT_WIDTH, DEEPNORM_BETA),
        'w_conv_in': dense(ks[16], (n_odd, D_MODEL, 3 * CONV_WIDTH), D_MODEL),
        'conv_w': dense(ks[17], (n_odd, CONV_K, CONV_WIDTH), CONV_K),
        'w_conv_out': dense(ks[18], (n_odd, CONV_WIDTH, D_MODEL), CONV_WIDTH, DEEPNORM_BETA),
        'w_router': dense(ks[19], (DEPTH, D_MODEL, N_EXPERTS), D_MODEL),
        'w_exp_gate': dense(ks[20], (DEPTH, N_EXPERTS, D_MODEL, EXPERT_FF), D_MODEL),
        'w_exp_up': dense(ks[21], (DEPTH, N_EXPERTS, D_MODEL, EXPERT_FF), D_MODEL),
        'w_exp_down': dense(ks[22], (DEPTH, N_EXPERTS, EXPERT_FF, D_MODEL), EXPERT_FF, DEEPNORM_BETA),
    }

def first_block(x, c, ctx, c_ctx, w_mod, b_mod, ln_mix_g, ln_mix_b, ln_ffn_g, ln_ffn_b,
              w_mix_in, q_norm_g, k_norm_g, w_pool_grp, pool_scale, w_mix_out,
              w_conv_in, conv_w, w_conv_out,
              w_router, w_exp_gate, w_exp_up, w_exp_down):
    rows = x.shape[1] // GRID_W
    cos, sin = _axial_rope_tables(rows)
    cond_lat = jax.nn.silu(c)
    cond_ctx = jax.nn.silu(c_ctx)[None, :]
    h_lat, h_ctx = x, ctx
    for layer in range(DEPTH):
        is_even = layer % 2 == 0
        ctx_out = any(j % 2 == 0 for j in range(layer + 1, DEPTH))
        ctx_in = is_even or ctx_out
        m_lat = _modulation(cond_lat, w_mod[layer], b_mod[layer])
        u_lat = _modulate(h_lat, m_lat[0], m_lat[1])
        u_ctx = None
        if ctx_in:
            m_ctx = _modulation(cond_ctx, w_mod[layer], b_mod[layer])
            u_ctx = _modulate(h_ctx, m_ctx[0], m_ctx[1])
        if is_even:
            e = layer // 2
            y_lat, y_ctx = _attn_pool_mixer(u_lat, u_ctx, cos, sin, w_mix_in[e], q_norm_g[e], k_norm_g[e],
                                            w_pool_grp[e], pool_scale[e], w_mix_out[e], ctx_out)
        else:
            o = layer // 2
            y_lat = _short_conv_mixer(u_lat, w_conv_in[o], conv_w[o], w_conv_out[o])
            y_ctx = _short_conv_mixer(u_ctx, w_conv_in[o], conv_w[o], w_conv_out[o]) if ctx_out else None
        h_lat = _post_norm(h_lat, m_lat[2] * y_lat, ln_mix_g[layer], ln_mix_b[layer])
        f_lat = _expert_choice_ffn(_modulate(h_lat, m_lat[3], m_lat[4]), w_router[layer],
                                   w_exp_gate[layer], w_exp_up[layer], w_exp_down[layer])
        h_lat = _post_norm(h_lat, m_lat[5] * f_lat, ln_ffn_g[layer], ln_ffn_b[layer])
        if ctx_out:
            h_ctx = _post_norm(h_ctx, m_ctx[2] * y_ctx, ln_mix_g[layer], ln_mix_b[layer])
            f_ctx = _expert_choice_ffn(_modulate(h_ctx, m_ctx[3], m_ctx[4]), w_router[layer],
                                       w_exp_gate[layer], w_exp_up[layer], w_exp_down[layer])
            h_ctx = _post_norm(h_ctx, m_ctx[5] * f_ctx, ln_ffn_g[layer], ln_ffn_b[layer])
    return h_lat


LRU_WIDTH = D_MODEL // 2
LRU_BLOCKS = 8
LRU_BLOCK = LRU_WIDTH // LRU_BLOCKS
CONV_WIDTH_2 = 4
LRU_C = 8.0
RET_HEADS = 8
RET_DIM = 64
RET_WIDTH = RET_HEADS * RET_DIM
RET_CHUNK = 128
RET_THETA = 10000.0
AB_IN = 2 * LRU_WIDTH + 4 * RET_WIDTH
AB_OUT = LRU_WIDTH + RET_WIDTH

NSA_HEADS = 16
NSA_KV_GROUPS = 4
NSA_HEAD_DIM = 64
NSA_REP = NSA_HEADS // NSA_KV_GROUPS
KV_WIDTH_2 = NSA_KV_GROUPS * NSA_HEAD_DIM
CMP_LEN = 32
CMP_STRIDE = 16
SLC_LEN = 64
SLC_TOPK = 16
WINDOW = 512
NSA_QBLOCK = 32
ROPE_THETA_2 = 500000.0
ROT_DIM = NSA_HEAD_DIM // 4
NSA_IN = NSA_HEADS * NSA_HEAD_DIM + 6 * KV_WIDTH_2 + 3 * NSA_HEADS

FFN_HIDDEN = ((8 * D_MODEL // 3 + 255) // 256) * 256

EPS = 1e-6
NEG = -1e30
BIG = 1e30
N_EVEN = (DEPTH + 1) // 2
N_ODD = DEPTH // 2


def rmsnorm(x, g):
    xf = x.astype(jnp.float32)
    y = xf * lax.rsqrt(jnp.mean(xf * xf, axis=-1, keepdims=True) + EPS)
    return (y * g.astype(jnp.float32)).astype(x.dtype)

def rotary(x, pos, rot_dim, theta):
    half = rot_dim // 2
    inv = theta ** (-jnp.arange(0, rot_dim, 2, dtype=jnp.float32) / rot_dim)
    ang = jnp.asarray(pos).astype(jnp.float32)[:, None] * inv
    cos = jnp.cos(ang)[:, None, :]
    sin = jnp.sin(ang)[:, None, :]
    x1 = x[..., :half].astype(jnp.float32)
    x2 = x[..., half:rot_dim].astype(jnp.float32)
    rot = jnp.concatenate([x1 * cos - x2 * sin, x2 * cos + x1 * sin], axis=-1).astype(x.dtype)
    return jnp.concatenate([rot, x[..., rot_dim:]], axis=-1)

def swiglu(x, w1, w3, w2):
    return (jax.nn.silu(x @ w1) * (x @ w3)) @ w2

def causal_depthwise_conv(x, w, b):
    S = x.shape[1]
    xp = jnp.pad(x, ((0, 0), (CONV_WIDTH_2 - 1, 0), (0, 0)))
    out = b
    for k in range(CONV_WIDTH_2):
        out = out + xp[:, k:k + S] * w[k]
    return out

def block_diag_linear(x, w, b):
    B, S, _ = x.shape
    xb = x.reshape(B, S, LRU_BLOCKS, LRU_BLOCK)
    return jnp.einsum('bsni,nij->bsnj', xb, w).reshape(B, S, LRU_WIDTH) + b

def rg_lru(x, ga_w, ga_b, gx_w, gx_b, lam):
    r = jax.nn.sigmoid(block_diag_linear(x, ga_w, ga_b)).astype(jnp.float32)
    i = jax.nn.sigmoid(block_diag_linear(x, gx_w, gx_b))
    log_a = -LRU_C * r * jax.nn.softplus(-lam.astype(jnp.float32))
    a = jnp.exp(log_a)
    mult = jnp.sqrt(-jnp.expm1(2.0 * log_a))
    u = mult * (i * x).astype(jnp.float32)

    def combine(left, right):
        a1, b1 = left
        a2, b2 = right
        return a1 * a2, a2 * b1 + b2

    _, h = lax.associative_scan(combine, (a, u), axis=1)
    return h.astype(x.dtype)

def retention(q, k, v):
    B, S, H, d = q.shape
    C = RET_CHUNK
    N = S // C
    pos = jnp.arange(S)
    q = rotary(q, pos, d, RET_THETA)
    k = rotary(k, pos, d, RET_THETA) * (d ** -0.5)
    log_g = jnp.log1p(-(2.0 ** (-5.0 - jnp.arange(H, dtype=jnp.float32))))
    ci = jnp.arange(C, dtype=jnp.float32)
    diff = ci[:, None] - ci[None, :]
    inner_decay = jnp.where(diff >= 0, jnp.exp(jnp.maximum(diff, 0.0) * log_g[:, None, None]), 0.0)
    q_decay = jnp.exp((ci + 1.0) * log_g[:, None])
    k_decay = jnp.exp((C - 1.0 - ci) * log_g[:, None])
    chunk_decay = jnp.exp(C * log_g)

    def to_chunks(t):
        return t.reshape(B, N, C, H, d).transpose(1, 0, 3, 2, 4)

    def step(state, inp):
        qi, ki, vi = inp
        qf, kf, vf = qi.astype(jnp.float32), ki.astype(jnp.float32), vi.astype(jnp.float32)
        s = jnp.einsum('bhid,bhjd->bhij', qf, kf) * inner_decay
        o = jnp.einsum('bhij,bhjd->bhid', s, vf) + jnp.einsum('bhid,bhde->bhie', qf * q_decay[..., None], state)
        state = state * chunk_decay[:, None, None] + jnp.einsum('bhjd,bhje->bhde', kf * k_decay[..., None], vf)
        return state, o

    state0 = jnp.zeros((B, H, d, d), jnp.float32)
    _, o = lax.scan(step, state0, (to_chunks(q), to_chunks(k), to_chunks(v)))
    o = o.transpose(1, 0, 3, 2, 4).reshape(B, S, H, d)
    mu = jnp.mean(o, axis=-1, keepdims=True)
    var = jnp.mean(jnp.square(o - mu), axis=-1, keepdims=True)
    return ((o - mu) * lax.rsqrt(var + EPS)).astype(v.dtype)

def hybrid_ab(h, w_in, conv_w, conv_b, ga_w, ga_b, gx_w, gx_b, lam, w_out):
    B, S, _ = h.shape
    proj = h @ w_in
    L, R = LRU_WIDTH, RET_WIDTH
    y, xr, q, k, v, g = jnp.split(proj, [L, 2 * L, 2 * L + R, 2 * L + 2 * R, 2 * L + 3 * R], axis=-1)
    xr = causal_depthwise_conv(xr, conv_w, conv_b)
    lru_out = rg_lru(xr, ga_w, ga_b, gx_w, gx_b, lam) * jax.nn.gelu(y)
    shp = (B, S, RET_HEADS, RET_DIM)
    ret = retention(q.reshape(shp), k.reshape(shp), v.reshape(shp)).reshape(B, S, R)
    ret_out = ret * jax.nn.silu(g)
    return jnp.concatenate([lru_out, ret_out], axis=-1) @ w_out

def nsa(h, w_in, pe_k, k_w1, k_w2, pe_v, v_w1, v_w2, w_out):
    B, S, _ = h.shape
    H, G, Rr, dh, QB = NSA_HEADS, NSA_KV_GROUPS, NSA_REP, NSA_HEAD_DIM, NSA_QBLOCK
    HD = H * dh
    proj = h @ w_in
    q = proj[..., :HD].reshape(B, S, H, dh)
    kv = proj[..., HD:HD + 6 * KV_WIDTH_2].reshape(B, S, 6, G, dh)
    k_cmp, v_cmp, k_slc, v_slc, k_win, v_win = [kv[:, :, j] for j in range(6)]
    gates = jax.nn.sigmoid(proj[..., HD + 6 * KV_WIDTH_2:].reshape(B, S, H, 3))
    pos = jnp.arange(S)
    q = rotary(q, pos, ROT_DIM, ROPE_THETA_2) * (dh ** -0.5)
    k_slc = rotary(k_slc, pos, ROT_DIM, ROPE_THETA_2)
    k_win = rotary(k_win, pos, ROT_DIM, ROPE_THETA_2)

    n_cmp = (S - CMP_LEN) // CMP_STRIDE + 1
    blk_idx = np.arange(n_cmp)[:, None] * CMP_STRIDE + np.arange(CMP_LEN)[None, :]
    cmp_end_np = blk_idx[:, -1]
    cmp_end = jnp.asarray(cmp_end_np)

    def compress(t, pe, w1, w2):
        blocks = t[:, blk_idx] + pe[:, None, :]
        blocks = blocks.transpose(0, 1, 3, 2, 4).reshape(B, n_cmp, G, CMP_LEN * dh)
        return jax.nn.gelu(blocks @ w1) @ w2

    kc = rotary(compress(k_cmp, pe_k, k_w1, k_w2), cmp_end_np, ROT_DIM, ROPE_THETA_2)
    vc = compress(v_cmp, pe_v, v_w1, v_w2)

    n_slc = S // SLC_LEN
    c_start = blk_idx[:, 0][:, None]
    s_start = np.arange(n_slc)[None, :] * SLC_LEN
    overlap = np.clip(np.minimum(c_start + CMP_LEN, s_start + SLC_LEN) - np.maximum(c_start, s_start), 0, None) / CMP_LEN
    cmp_to_slc = jnp.asarray(overlap, jnp.float32)
    top_k = min(SLC_TOPK, n_slc)
    ks_blocks = k_slc.reshape(B, n_slc, SLC_LEN, G, dh).transpose(0, 3, 1, 2, 4)
    vs_blocks = v_slc.reshape(B, n_slc, SLC_LEN, G, dh).transpose(0, 3, 1, 2, 4)
    gather = jax.vmap(jax.vmap(lambda blocks, idx: blocks[idx]))
    kw_pad = jnp.pad(k_win, ((0, 0), (WINDOW, 0), (0, 0), (0, 0)))
    vw_pad = jnp.pad(v_win, ((0, 0), (WINDOW, 0), (0, 0), (0, 0)))
    blk = jnp.arange(n_slc)

    def attend_block(qi):
        t0 = qi * QB
        qpos = t0 + jnp.arange(QB)
        qb = lax.dynamic_slice_in_dim(q, t0, QB, axis=1).reshape(B, QB, G, Rr, dh)
        s = jnp.einsum('bqgrd,bngd->bgrqn', qb, kc).astype(jnp.float32)
        vis = cmp_end[None, :] <= qpos[:, None]
        p_cmp = jnp.where(vis, jax.nn.softmax(jnp.where(vis, s, NEG), axis=-1), 0.0)
        o_cmp = jnp.einsum('bgrqn,bngd->bqgrd', p_cmp.astype(vc.dtype), vc)
        imp = jnp.einsum('bgrqn,nj->bgqj', p_cmp, cmp_to_slc)
        cur = qpos[:, None] // SLC_LEN
        forced = (blk[None, :] == 0) | (blk[None, :] == cur) | (blk[None, :] == cur - 1)
        causal_blk = blk[None, :] * SLC_LEN <= qpos[:, None]
        imp = jnp.where(forced, BIG, jnp.where(causal_blk, imp, NEG))
        _, sel = lax.top_k(imp, top_k)
        kg = gather(ks_blocks, sel)
        vg = gather(vs_blocks, sel)
        s = jnp.einsum('bqgrd,bgqkld->bgrqkl', qb, kg).astype(jnp.float32)
        tok = sel[..., None] * SLC_LEN + jnp.arange(SLC_LEN)
        ok = tok <= qpos[:, None, None]
        s = jnp.where(ok[:, :, None], s, NEG).reshape(B, G, Rr, QB, top_k * SLC_LEN)
        p_slc = jax.nn.softmax(s, axis=-1).reshape(B, G, Rr, QB, top_k, SLC_LEN)
        o_slc = jnp.einsum('bgrqkl,bgqkld->bqgrd', p_slc.astype(vg.dtype), vg)
        kw = lax.dynamic_slice_in_dim(kw_pad, t0, WINDOW + QB, axis=1)
        vw = lax.dynamic_slice_in_dim(vw_pad, t0, WINDOW + QB, axis=1)
        kpos = t0 - WINDOW + jnp.arange(WINDOW + QB)
        dist = qpos[:, None] - kpos[None, :]
        band = (dist >= 0) & (dist < WINDOW) & (kpos[None, :] >= 0)
        s = jnp.einsum('bqgrd,bkgd->bgrqk', qb, kw).astype(jnp.float32)
        p_win = jax.nn.softmax(jnp.where(band, s, NEG), axis=-1)
        o_win = jnp.einsum('bgrqk,bkgd->bqgrd', p_win.astype(vw.dtype), vw)
        gb = lax.dynamic_slice_in_dim(gates, t0, QB, axis=1).reshape(B, QB, G, Rr, 3)
        o = gb[..., 0:1] * o_cmp + gb[..., 1:2] * o_slc + gb[..., 2:3] * o_win
        return o.reshape(B, QB, HD)

    out = lax.map(attend_block, jnp.arange(S // QB))
    out = out.transpose(1, 0, 2, 3).reshape(B, S, HD)
    return out @ w_out

def second_inputs(seed: int = 0) -> dict:
    key = jax.random.key(seed)
    ks = jax.random.split(key, 24)
    f32 = jnp.float32

    def w(k, shape, fan_in):
        return jax.random.normal(k, shape, f32) * (fan_in ** -0.5)

    def gain(k, shape):
        return 1.0 + 0.01 * jax.random.normal(k, shape, f32)

    a_pow_c = jax.random.uniform(ks[9], (N_EVEN, LRU_WIDTH), f32, 0.9, 0.999)
    root = a_pow_c ** (1.0 / LRU_C)
    lru_lambda = jnp.log(root) - jnp.log1p(-root)
    return {
        'x': jax.random.normal(ks[0], (BATCH, SEQ, D_MODEL), f32),
        'attn_norm': gain(ks[1], (DEPTH, D_MODEL)),
        'ab_w_in': w(ks[2], (N_EVEN, D_MODEL, AB_IN), D_MODEL),
        'conv_w': w(ks[3], (N_EVEN, CONV_WIDTH_2, LRU_WIDTH), CONV_WIDTH_2),
        'conv_b': 0.01 * jax.random.normal(ks[4], (N_EVEN, LRU_WIDTH), f32),
        'gate_a_w': w(ks[5], (N_EVEN, LRU_BLOCKS, LRU_BLOCK, LRU_BLOCK), LRU_BLOCK),
        'gate_a_b': 0.01 * jax.random.normal(ks[6], (N_EVEN, LRU_WIDTH), f32),
        'gate_x_w': w(ks[7], (N_EVEN, LRU_BLOCKS, LRU_BLOCK, LRU_BLOCK), LRU_BLOCK),
        'gate_x_b': 0.01 * jax.random.normal(ks[8], (N_EVEN, LRU_WIDTH), f32),
        'lru_lambda': lru_lambda,
        'ab_w_out': w(ks[10], (N_EVEN, AB_OUT, D_MODEL), AB_OUT),
        'nsa_w_in': w(ks[11], (N_ODD, D_MODEL, NSA_IN), D_MODEL),
        'cmp_pe_k': 0.02 * jax.random.normal(ks[12], (N_ODD, CMP_LEN, NSA_HEAD_DIM), f32),
        'cmp_k_w1': w(ks[13], (N_ODD, CMP_LEN * NSA_HEAD_DIM, NSA_HEAD_DIM), CMP_LEN * NSA_HEAD_DIM),
        'cmp_k_w2': w(ks[14], (N_ODD, NSA_HEAD_DIM, NSA_HEAD_DIM), NSA_HEAD_DIM),
        'cmp_pe_v': 0.02 * jax.random.normal(ks[15], (N_ODD, CMP_LEN, NSA_HEAD_DIM), f32),
        'cmp_v_w1': w(ks[16], (N_ODD, CMP_LEN * NSA_HEAD_DIM, NSA_HEAD_DIM), CMP_LEN * NSA_HEAD_DIM),
        'cmp_v_w2': w(ks[17], (N_ODD, NSA_HEAD_DIM, NSA_HEAD_DIM), NSA_HEAD_DIM),
        'nsa_w_out': w(ks[18], (N_ODD, NSA_HEADS * NSA_HEAD_DIM, D_MODEL), NSA_HEADS * NSA_HEAD_DIM),
        'ffn_norm': gain(ks[19], (DEPTH, D_MODEL)),
        'ffn_w1': w(ks[20], (DEPTH, D_MODEL, FFN_HIDDEN), D_MODEL),
        'ffn_w3': w(ks[21], (DEPTH, D_MODEL, FFN_HIDDEN), D_MODEL),
        'ffn_w2': w(ks[22], (DEPTH, FFN_HIDDEN, D_MODEL), FFN_HIDDEN),
        'final_norm': gain(ks[23], (D_MODEL,)),
    }

def second_block(x, attn_norm, ab_w_in, conv_w, conv_b, gate_a_w, gate_a_b, gate_x_w, gate_x_b,
              lru_lambda, ab_w_out, nsa_w_in, cmp_pe_k, cmp_k_w1, cmp_k_w2, cmp_pe_v, cmp_v_w1,
              cmp_v_w2, nsa_w_out, ffn_norm, ffn_w1, ffn_w3, ffn_w2, final_norm):
    h = x
    for layer in range(DEPTH):
        hn = rmsnorm(h, attn_norm[layer])
        i = layer // 2
        if layer % 2 == 0:
            h = h + hybrid_ab(hn, ab_w_in[i], conv_w[i], conv_b[i], gate_a_w[i], gate_a_b[i],
                              gate_x_w[i], gate_x_b[i], lru_lambda[i], ab_w_out[i])
        else:
            h = h + nsa(hn, nsa_w_in[i], cmp_pe_k[i], cmp_k_w1[i], cmp_k_w2[i],
                        cmp_pe_v[i], cmp_v_w1[i], cmp_v_w2[i], nsa_w_out[i])
        h = h + swiglu(rmsnorm(h, ffn_norm[layer]), ffn_w1[layer], ffn_w3[layer], ffn_w2[layer])
    return rmsnorm(h, final_norm)


def setup_inputs(seed=0):
    out = dict(first_inputs(seed))
    for name, value in second_inputs(seed + 1).items():
        if name != "x":
            out[name + "_2"] = value
    return out


def reference(
    x, c, ctx, c_ctx, w_mod, b_mod, ln_mix_g, ln_mix_b, ln_ffn_g, ln_ffn_b, w_mix_in, q_norm_g,
    k_norm_g, w_pool_grp, pool_scale, w_mix_out, w_conv_in, conv_w, w_conv_out, w_router,
    w_exp_gate, w_exp_up, w_exp_down, attn_norm_2, ab_w_in_2, conv_w_2, conv_b_2, gate_a_w_2,
    gate_a_b_2, gate_x_w_2, gate_x_b_2, lru_lambda_2, ab_w_out_2, nsa_w_in_2, cmp_pe_k_2,
    cmp_k_w1_2, cmp_k_w2_2, cmp_pe_v_2, cmp_v_w1_2, cmp_v_w2_2, nsa_w_out_2, ffn_norm_2,
    ffn_w1_2, ffn_w3_2, ffn_w2_2, final_norm_2,
):
    x = first_block(
        x, c, ctx, c_ctx, w_mod, b_mod, ln_mix_g, ln_mix_b, ln_ffn_g, ln_ffn_b, w_mix_in,
        q_norm_g, k_norm_g, w_pool_grp, pool_scale, w_mix_out, w_conv_in, conv_w, w_conv_out,
        w_router, w_exp_gate, w_exp_up, w_exp_down,
    )
    return second_block(
        x, attn_norm_2, ab_w_in_2, conv_w_2, conv_b_2, gate_a_w_2, gate_a_b_2, gate_x_w_2,
        gate_x_b_2, lru_lambda_2, ab_w_out_2, nsa_w_in_2, cmp_pe_k_2, cmp_k_w1_2, cmp_k_w2_2,
        cmp_pe_v_2, cmp_v_w1_2, cmp_v_w2_2, nsa_w_out_2, ffn_norm_2, ffn_w1_2, ffn_w3_2,
        ffn_w2_2, final_norm_2,
    )


_drawn_inputs = setup_inputs


def setup_inputs(seed=0):
    import zlib

    import numpy as np

    out = dict(_drawn_inputs(seed))
    spreads = {}
    factors = {'ctx': 8.0,
     'c_ctx': 3.017,
     'b_mod': 5.708,
     'q_norm_g': 8.0,
     'k_norm_g': 8.0,
     'pool_scale': 8.0,
     'attn_norm_2': 5.291,
     'gate_a_b_2': 8.0,
     'gate_x_b_2': 8.0,
     'cmp_pe_k_2': 64.0,
     'cmp_pe_v_2': 64.0,
     'ffn_norm_2': 5.931,
     'final_norm_2': 32.632}
    for name, (base, spread) in spreads.items():
        noise = np.random.default_rng([zlib.crc32(name.encode()), seed]).standard_normal(out[name].shape)
        drawn = base * np.exp(spread * noise) if base else spread * noise
        out[name] = __import__('jax').numpy.asarray(drawn.astype(out[name].dtype))
    for name, factor in factors.items():
        out[name] = (out[name] * factor).astype(out[name].dtype)
    return out
```

```python
from contextlib import ExitStack

import numpy as np

import concourse.bass as bass
from concourse import mybir

F32 = mybir.dt.float32
ALU = mybir.AluOpType
ACT = mybir.ActivationFunctionType
AX = mybir.AxisListType.X

P = 128
D = 1024
S = 512
NT = S // P
NC = D // P
CTX = 256
DH = 64
E = 16
CAP = 2 * S // E
FF = ((8 * D // 3 + 255) // 256) * 256
NF = FF // P
EPS = 1e-6
ALPHA = 4.0 ** 0.25
NEG = -1e30
N_CMP = (S - 32) // 16 + 1
HALF = 512
SLOT = 4096
N_SLOTS = 5



class Token:

    def __init__(self, line):
        self.line, self.named, self.value = line, False, 0

    def point(self):
        return self.line.sem, self.value


class Landed:

    def __init__(self, sem, value):
        self.sem, self.value = sem, value

    def point(self):
        return self.sem, self.value


class Line:

    def __init__(self, sem, chained):
        self.sem, self.chained, self.items, self.last = sem, chained, [], None
        self.fence = []

    def waits_once(self, after):
        self.fence = self.fence + list(after)

    def waits(self, after):
        after = [t for t in after if t is not None] + self.fence
        self.fence = []
        return after

    def __call__(self, issue, *args, after=(), **kw):
        after = self.waits(after)
        if self.chained and self.last is not None:
            after.append(self.last)
        for t in after:
            if isinstance(t, Token):
                t.named = True
        done = Token(self)
        self.items.append((after, issue, args, kw, done))
        self.last = done
        return done

    def dma(self, issue, out, in_, count, after=()):
        after = self.waits(after)
        for t in after:
            if isinstance(t, Token):
                t.named = True
        count[1] += 16
        done = Landed(count[0], count[1])
        self.items.append((after, issue, (out, in_), {}, done))
        return done

    def number(self):
        n = 0
        for *_, done in self.items:
            if isinstance(done, Token) and done.named:
                n += 1
                done.value = n

    def emit(self, eng):
        reached = {}
        for after, issue, args, kw, done in self.items:
            need = {}
            for t in after:
                sem, value = t.point()
                if value > need.get(id(sem), (sem, 0))[1]:
                    need[id(sem)] = (sem, value)
            for key, (sem, value) in need.items():
                if reached.get(key, 0) < value:
                    eng.wait_ge(sem, value)
                    reached[key] = value
            ins = issue(*args, **kw)
            if isinstance(done, Landed):
                ins.then_inc(done.sem, 16)
            elif done.named:
                ins.then_inc(self.sem, 1)


class Bank:
    def __init__(self, ap):
        self.ap, self.readers = ap, []

    def free(self, token):
        self.readers.append(token)


class Banks:

    def __init__(self, ap):
        self.ap = ap
        self.banks = [Bank(ap[:, i, :]) for i in range(8)]
        self.at = 0

    def take(self):
        b = self.banks[self.at % 8]
        self.at += 1
        b.wait, b.readers = b.readers, []
        return b

    def take_run(self, n):
        while self.at % n:
            self.at += 1
        got = [self.take() for _ in range(n)]
        i = (self.at - n) % 8
        run = Bank(self.ap[:, i:i + n, :])
        run.wait = [t for b in got for t in b.wait]

        def free(token):
            for b in got:
                b.free(token)
        run.free = free
        return run


class Arena:

    def __init__(self, ap, words):
        self.ap, self.words, self.at = ap, words, 0

    def __call__(self, *shape):
        n = int(np.prod(shape))
        assert self.at + n <= self.words, (self.at, n, self.words)
        v = self.ap[:, self.at:self.at + n]
        self.at += n + (n % 2)
        if len(shape) == 2:
            v = v.rearrange("p (a b) -> p a b", a=shape[0])
        elif len(shape) == 3:
            v = v.rearrange("p (a b c) -> p a b c", a=shape[0], b=shape[1])
        return v


class Piece:
    def __init__(self, ap, landed, slot):
        self.ap, self.landed, self.slot = ap, landed, slot

    def done(self, token):
        self.slot["readers"] = [token]


def shape_constants():
    f = np.float32
    tok = np.arange(S)

    def rope(pos, inv):
        ang = pos.astype(f)[:, None] * inv.astype(f)
        return np.cos(ang).astype(f), np.sin(ang).astype(f)

    def tiles(a):
        return np.ascontiguousarray(a.reshape(-1, P, a.shape[1]).transpose(1, 0, 2))

    c = {}
    c["ident"] = np.eye(P, dtype=f)
    sum_cols = np.zeros((P, 2), f)
    sum_rows = np.zeros((P, P), f)
    for g in range(4):
        sum_cols[32 * g, 0] = sum_cols[32 * g + 1, 1] = 1
        sum_rows[32 * g, :] = 1
    c["sum_cols"], c["sum_rows"] = sum_cols, sum_rows
    c["slot_ids"] = np.broadcast_to(np.arange(1, CAP + 1, dtype=f), (P, CAP)).copy()
    c["ones"] = np.ones((E, S), f)
    q = np.arange(P)
    c["causal"] = np.where(q[None, :] <= q[:, None], 0, NEG).astype(f)
    ends = np.arange(N_CMP) * 16 + 31
    seen = (ends[None, :] <= tok[:, None])
    c["cmp_seen"] = tiles(seen.astype(f))
    c["cmp_hide"] = tiles(np.where(seen, 0, NEG).astype(f))
    inv = f(10000.0) ** (-np.arange(0, 32, 2, dtype=f) / f(32))
    row_c, row_s = rope(tok // 64, inv)
    col_c, col_s = rope(tok % 64, inv)
    c["ax_cos"], c["ax_sin"] = tiles(np.concatenate([row_c, col_c], 1)), tiles(np.concatenate([row_s, col_s], 1))
    a, b = rope(tok, f(10000.0) ** (-np.arange(0, 64, 2, dtype=f) / f(64)))
    c["ret_cos"], c["ret_sin"] = tiles(a), tiles(b)
    inv = f(500000.0) ** (-np.arange(0, 16, 2, dtype=f) / f(16))
    a, b = rope(tok, inv)
    c["nsa_cos"], c["nsa_sin"] = tiles(a), tiles(b)
    c["cmp_cos"], c["cmp_sin"] = rope(ends, inv)
    counts = np.stack([np.minimum(tok + w // 2, S) - np.maximum(tok - w // 2, 0) for w in (2, 4, 8, 16)])
    c["pool_inv"] = np.broadcast_to((1.0 / counts).astype(f), (P, 4, S)).copy()
    log_g = np.log1p(-(2.0 ** (-5.0 - np.arange(8))))
    diff = np.arange(S)[None, :] - np.arange(P)[:, None]
    dec = np.where(diff[None] >= 0, np.exp(np.maximum(diff, 0)[None] * log_g[:, None, None]), 0.0)
    c["decay"] = np.ascontiguousarray(dec.transpose(1, 0, 2)).astype(f)
    return c



class Core:

    def __init__(self, nc, ctx, dram):
        self.nc, self.dram = nc, dram

        def sem(name):
            return ctx.enter_context(nc.semaphore(name))

        def sbuf(name, shape):
            return ctx.enter_context(nc.sbuf_tensor(name, shape, F32))

        self.pe = Line(sem("pe_done"), chained=False)
        self.dve = Line(sem("dve_done"), chained=True)
        self.act = Line(sem("act_done"), chained=True)
        self.pool = Line(sem("pool_done"), chained=True)
        self.sync = Line(sem("sync_done"), chained=False)
        self.banks = Banks(ctx.enter_context(nc.psum_tensor("psum", [P, 8, HALF], F32))[:, :, :])
        ring = sbuf("weight_ring", [P, N_SLOTS, SLOT])
        self.slots = [dict(ap=ring[:, i, :], count=[sem(f"slot{i}_landed"), 0], readers=[])
                      for i in range(N_SLOTS)]
        self.next_slot = 0
        self.new_sem, self.n_loads = sem, 0
        self.h = sbuf("h", [P, NT, D])
        self.consts = sbuf("consts", [P, 2 * P + CAP + 2])
        self.ident = self.consts[:, 0:P]
        self.sum_rows = self.consts[:, P:2 * P]
        self.slot_ids = self.consts[:, 2 * P:2 * P + CAP]
        self.sum_cols = self.consts[:, 2 * P + CAP:2 * P + CAP + 2]
        words = (nc.sbuf_bytes_remaining - 64) // 4
        self.arena = Arena(sbuf("arena", [P, words]), words)
        self.flip = 0
        self.out_count = [sem("out_landed"), 0]

    def weights(self, src):
        chunks, cols = src.shape[1], src.shape[2]
        slot = self.slots[self.next_slot % N_SLOTS]
        self.next_slot += 1
        assert slot["readers"] is not None and chunks * cols <= SLOT
        view = slot["ap"][:, 0:chunks * cols].rearrange("p (c n) -> p c n", c=chunks)
        landed = self.sync.dma(self.nc.sync.dma_start, view, src, slot["count"], after=slot["readers"])
        slot["readers"] = None
        return Piece(view, landed, slot)

    def loads(self, pairs, after=()):
        count = [self.new_sem(f"load{self.n_loads}_landed"), 0]
        self.n_loads += 1
        self.pool.waits_once(after)
        for out, in_ in pairs:
            t = self.pool.dma(self.nc.gpsimd.dma_start, out, in_, count)
        return t

    def barrier(self):
        lines = [self.pe, self.dve, self.act, self.pool]
        for line in lines:
            line.fence = line.fence + [o.last for o in lines if o.last is not None and (o is not line or o is self.pool)]

    def mm(self, out, lhsT, rhs, start=True, stop=True, after=()):
        return self.pe(self.nc.tensor.matmul, out, lhsT, rhs, start=start, stop=stop, after=after)

    def tr(self, out, in_, after=()):
        k = in_.shape[0]
        return self.pe(self.nc.tensor.transpose, out, in_, self.ident[0:k, 0:k], after=after)

    def tt(self, out, a, b, op, after=()):
        return self.dve(self.nc.vector.tensor_tensor, out, a, b, op, after=after)

    def ts(self, out, a, s1, s2, op0, op1=None, after=()):
        if op1 is None:
            return self.dve(self.nc.vector.tensor_scalar, out, a, s1, None, op0, after=after)
        return self.dve(self.nc.vector.tensor_scalar, out, a, s1, s2, op0, op1, after=after)

    def stt(self, out, a, s, b, op0, op1, after=()):
        return self.dve(self.nc.vector.scalar_tensor_tensor, out, a, s, b, op0, op1, after=after)

    def act_fn(self, out, in_, fn, after=(), **kw):
        return self.act(self.nc.scalar.activation, out, in_, fn, after=after, **kw)

    def evac(self, out, in_, after=()):
        self.flip ^= 1
        if self.flip:
            return self.act_fn(out, in_, ACT.Copy, after=after)
        return self.dve(self.nc.vector.tensor_copy, out, in_, after=after)



def rows(w, c0, c1, n0, n1):
    return w[c0 * P:c1 * P, n0:n1].rearrange("(c p) n -> p c n", p=P)


def project_features(k, w, n0, n1, xT, use, ready=(), width=S):
    for m0 in range(n0, n1, HALF):
        m1 = min(m0 + HALF, n1)
        piece = k.weights(rows(w, 0, NC, m0, m1))
        for m in range(m0, m1, P):
            bank = k.banks.take()
            for c in range(NC):
                t = k.mm(bank.ap[:, 0:width], piece.ap[:, c, m - m0:m - m0 + P], xT(c), c == 0, c == NC - 1,
                         after=[piece.landed, *bank.wait, *ready] if c == 0 else ())
            if m + P >= m1:
                piece.done(t)
            use((m - n0) // P, bank, t)


def project_tokens(k, w, n0, n1, xT, use, ready=(), tiles=NT, more=None):
    piece = k.weights(rows(w, 0, NC, n0, n1))
    for x, n, u in [(xT, tiles, use)] + ([more] if more else []):
        for t in range(n):
            bank = k.banks.take()
            for c in range(NC):
                tok = k.mm(bank.ap[:, 0:n1 - n0], x(c)[:, t * P:(t + 1) * P], piece.ap[:, c, :], c == 0, c == NC - 1,
                           after=[piece.landed, *bank.wait, *ready] if c == 0 else ())
            if t == n - 1:
                piece.done(tok)
                piece_last = tok
            u(t, bank, tok)
    piece.done(piece_last)


def project_out(k, w, xT, use, ready=()):
    pieces = [k.weights(rows(w, 0, NC, half * HALF, (half + 1) * HALF)) for half in range(2)]
    for t in range(NT):
        for half, piece in enumerate(pieces):
            bank = k.banks.take()
            for c in range(NC):
                tok = k.mm(bank.ap, xT(c)[:, t * P:(t + 1) * P], piece.ap[:, c, :], c == 0, c == NC - 1,
                           after=[piece.landed, *bank.wait, *ready] if c == 0 else ())
            if t == NT - 1:
                piece.done(tok)
            use(t, half, bank, tok)


def feature_major(k, src, dst, scale, shift, ready=()):
    for c in range(NC):
        bank = k.banks.take()
        for t in range(NT):
            tok = k.tr(bank.ap[:, t * P:(t + 1) * P], src[:, t, c * P:(c + 1) * P],
                       after=[*bank.wait, *ready] if t == 0 else ())
        if shift is None:
            done = k.ts(dst[:, c, :], bank.ap, scale[:, c:c + 1], None, ALU.mult, after=[tok])
        else:
            done = k.ts(dst[:, c, :], bank.ap, scale[:, c:c + 1], shift[:, c:c + 1], ALU.mult, ALU.add, after=[tok])
        bank.free(done)
    return done


def inverse_root(k, out, in_, scale, after=()):
    v = k.ts(out, in_, scale, EPS, ALU.mult, ALU.add, after=after)
    a = k.act_fn(out, out, ACT.Sqrt, after=[v])
    return k.dve(k.nc.vector.reciprocal, out, out, after=[a])



def modulation(k, layer, cond, m):
    cols, gates = m["cols"], m["gates"]
    bias_cols, gate_bias = m["bias_cols"], m["gate_bias"]
    part = [m["part"][:, i, :] for i in range(2)]
    part_read = [None, None]
    small = k.loads([(bias_cols, k.dram["b_mod_cols"][layer]),
                     *[(gate_bias[:, i, :], k.dram["b_mod"][layer, c * D:(c + 1) * D].partition_broadcast(P))
                       for i, c in enumerate((2, 5))]])
    pieces = 6 * D // HALF
    made = {}

    def add_partials(j):
        buf, tok = made.pop(j)
        bank = k.banks.take()
        chunk, half = j // 2, j % 2
        if chunk in (2, 5):
            t = k.mm(bank.ap, k.sum_rows, part[buf], after=[tok, *bank.wait])
            part_read[buf] = t
            done = k.tt(gates[:, chunk // 3, half * HALF:(half + 1) * HALF], bank.ap,
                        gate_bias[:, chunk // 3, half * HALF:(half + 1) * HALF], ALU.add, after=[t, small])
        else:
            for i in range(4):
                t = k.mm(bank.ap[:, 2 * i:2 * i + 2], part[buf][:, i * P:(i + 1) * P], k.sum_cols,
                         after=[tok, *bank.wait] if i == 0 else ())
            part_read[buf] = t
            done = k.tt(cols[:, 4 * j:4 * j + 4, :], bank.ap[:, 0:8].rearrange("p (a b) -> p a b", b=2),
                        bias_cols[:, 4 * j:4 * j + 4].unsqueeze(2).to_broadcast([P, 4, 2]), ALU.add,
                        after=[t, small])
        bank.free(done)
        return done

    for j in range(pieces):
        piece = k.weights(rows(k.dram["w_mod"][layer], 0, NC, j * HALF, (j + 1) * HALF))
        bank = k.banks.take()
        for r in range(2):
            for g in range(4):
                c = 4 * r + g
                t = k.mm(bank.ap[32 * g:32 * g + 32, :], cond[:, c, :], piece.ap[:, c, :], r == 0, r == 1,
                         after=[piece.landed, k.cond_ready, *bank.wait] if c == 0 else ())
        piece.done(t)
        buf = j % 2
        done = k.act_fn(part[buf], bank.ap, ACT.Copy, after=[t, part_read[buf]])
        bank.free(done)
        made[j] = (buf, done)
        if j:
            add_partials(j - 1)
    add_partials(pieces - 1)
    k.ts(cols[:, 8:16, :], cols[:, 8:16, :], 1.0, None, ALU.add)
    return k.ts(cols[:, 32:40, :], cols[:, 32:40, :], 1.0, None, ALU.add)


def post_norm(k, gate, gain, bias, ready):
    z = k.arena(2, D)
    st = k.arena(2, 2, 6)
    mv = k.arena(2, 2)
    r = k.arena(2, 1)
    last = []

    def use(t, half, bank, tok):
        b = t % 2
        zb = z[:, b, half * HALF:(half + 1) * HALF]
        done = k.tt(zb, bank.ap, gate[:, half * HALF:(half + 1) * HALF], ALU.mult, after=[tok, ready])
        bank.free(done)
        k.stt(zb, k.h[:, t, half * HALF:(half + 1) * HALF], ALPHA, zb, ALU.mult, ALU.add)
        k.dve(k.nc.vector.bn_stats, st[:, b, half, :], zb)
        if half:
            k.dve(k.nc.vector.bn_aggr, mv[:, b, :], st[:, b, :, :])
            inverse_root(k, r[:, b, :], mv[:, b, 1:2], 1.0)
            k.ts(z[:, b, :], z[:, b, :], mv[:, b, 0:1], r[:, b, :], ALU.subtract, ALU.mult)
            k.tt(z[:, b, :], z[:, b, :], gain, ALU.mult)
            last[:] = [k.tt(k.h[:, t, :], z[:, b, :], bias, ALU.add)]
    return use, last



def head_norm(k, src, heads, gain, tmp, small, out, after):
    sq = tmp[:, 0:heads * DH]
    a = k.act_fn(sq, src, ACT.Square, after=after)
    k.dve(k.nc.vector.tensor_reduce, small[:, 0:heads], sq.rearrange("p (h d) -> p h d", d=DH), AX, ALU.add, after=[a])
    inverse_root(k, small[:, 0:heads], small[:, 0:heads], 1.0 / DH)
    o = out.rearrange("p (h d) -> p h d", d=DH)
    if heads == 8:
        for kv in range(2):
            hs = slice(4 * kv, 4 * kv + 4)
            t = k.tt(out.rearrange("p (g kv d) -> p g kv d", g=4, kv=2)[:, :, kv, :],
                     src.rearrange("p (h d) -> p h d", d=DH)[:, hs, :],
                     small[:, hs].unsqueeze(2).to_broadcast([P, 4, DH]), ALU.mult)
    else:
        t = k.tt(o, src.rearrange("p (h d) -> p h d", d=DH), small[:, 0:heads].unsqueeze(2).to_broadcast([P, heads, DH]),
                 ALU.mult)
    last = k.tt(o, o, gain.unsqueeze(1).to_broadcast([P, heads, DH]), ALU.mult)
    return t, last


def rotate(k, x0, x1, out0, out1, cos, sin, tmp, shape, after=()):
    n, heads, half = shape
    c = cos.unsqueeze(1).to_broadcast([n, heads, half])
    s = sin.unsqueeze(1).to_broadcast([n, heads, half])
    a, b = [x.rearrange("p (h d) -> p h d", h=heads) for x in tmp]
    k.tt(a, x0, c, ALU.mult, after=after)
    k.tt(b, x1, s, ALU.mult)
    k.tt(a, a, b, ALU.subtract)
    k.tt(b, x0, s, ALU.mult)
    t = k.tt(out1, x1, c, ALU.mult)
    k.tt(out1, out1, b, ALU.add)
    return k.dve(k.nc.vector.tensor_copy, out0, a)


def softmax_rows(k, scores, n_heads, n, scale, out, stats, gate=None, after=(), out_free=(), keep=None):
    mx, sm = stats[:, 0, 0:n_heads], stats[:, 1, 0:n_heads]
    k.dve(k.nc.vector.tensor_reduce, mx, scores, AX, ALU.max, after=after)
    v = k.ts(mx, mx, -scale, None, ALU.mult)
    for i in range(n_heads):
        a = k.act_fn(out[:, i, 0:n], scores[:, i, :], ACT.Exp, bias=mx[:, i:i + 1], scale=scale,
                     accum_out=sm[:, i:i + 1], after=[v, *out_free])
    k.dve(k.nc.vector.reciprocal, sm, sm, after=[a])
    if gate is not None:
        k.tt(sm.rearrange("p (r g) -> p r g", g=2), sm.rearrange("p (r g) -> p r g", g=2), gate, ALU.mult)
    for i in range(n_heads):
        if keep is not None:
            last = k.stt(out[:, i, 0:n], out[:, i, 0:n], sm[:, i:i + 1], keep, ALU.mult, ALU.mult)
        else:
            last = k.ts(out[:, i, 0:n], out[:, i, 0:n], sm[:, i:i + 1], None, ALU.mult)
    return a, last



def attn_pool(k, m):
    d, nc = k.dram, k.nc
    cols = m["cols"]
    N_KEYS = CTX + S
    NK = N_KEYS // P
    catT = k.arena(NC, S)
    top = k.arena.at
    uT, ucT = k.arena(NC, S), k.arena(NC, CTX)
    qT, kT, v = k.arena(4, S), k.arena(N_KEYS), k.arena(NK, P)
    keep = k.arena.at
    cos, sin = k.arena(NT, 32), k.arena(NT, 32)
    gq, gk = k.arena(DH), k.arena(DH)
    inv, grp, p_scale = k.arena(4, S), k.arena(4, P), k.arena(4)
    landed = k.loads([(uT, d["xT"].rearrange("(c p) s -> p c s", p=P)),
                      (ucT, d["ctxT"].rearrange("(c p) s -> p c s", p=P))])
    small = k.loads([(cos, d["ax_cos"]), (sin, d["ax_sin"]),
                     (gq, d["q_norm_g"].partition_broadcast(P)), (gk, d["k_norm_g"].partition_broadcast(P)),
                     (inv, d["pool_inv"]), (grp, d["w_pool_grp"].rearrange("g c d -> c g d")),
                     (p_scale, d["pool_scale_cols"])])
    for c in range(NC):
        k.ts(uT[:, c, :], uT[:, c, :], cols[:, 8 + c, 0:1], cols[:, c, 0:1], ALU.mult, ALU.add, after=[landed])
        u_ready = k.ts(ucT[:, c, :], ucT[:, c, :], cols[:, 8 + c, 1:2], cols[:, c, 1:2], ALU.mult, ALU.add)

    tmp, st = k.arena(HALF), k.arena(8)
    qn, half = k.arena(HALF), k.arena(2, HALF // 2)
    rope_read = [None]

    def pairs(x):
        return x.rearrange("p (h d two) -> p h d two", two=2, d=DH // 2)

    def rope_tile(src, heads, gain, t, after):
        n = heads * DH
        read, last = head_norm(k, src, heads, gain, tmp, st, qn[:, 0:n], [*after, rope_read[0]])
        if t is not None:
            x = pairs(qn[:, 0:n])
            last = rotate(k, x[:, :, :, 0], x[:, :, :, 1], x[:, :, :, 0], x[:, :, :, 1], cos[:, t, :], sin[:, t, :],
                          [half[:, i, 0:n // 2] for i in range(2)], (P, heads, DH // 2))
        return read, last

    def use_q(t, bank, tok):
        read, last = rope_tile(bank.ap, 8, gq, t, [tok, small])
        bank.free(read)
        out = k.banks.take()
        for g in range(4):
            tt = k.tr(out.ap[:, g * P:(g + 1) * P], qn[:, g * P:(g + 1) * P], after=[last, *out.wait])
        rope_read[0] = tt
        e = k.evac(qT[:, :, t * P:(t + 1) * P], out.ap.rearrange("p (g q) -> p g q", g=4), after=[tt])
        out.free(e)

    def use_kv(first, is_ctx):
        def use(t, bank, tok):
            kt = first + t
            a = k.act_fn(v[:, kt, :], bank.ap[:, P:2 * P], ACT.Copy, after=[tok])
            read, last = rope_tile(bank.ap[:, 0:P], 2, gk, None if is_ctx else t, [tok, small])
            bank.free(read)
            bank.free(a)
            out = k.banks.take()
            tt = k.tr(out.ap[:, 0:P], qn[:, 0:P], after=[last, *out.wait])
            rope_read[0] = tt
            e = k.evac(kT[:, kt * P:(kt + 1) * P], out.ap[:, 0:P], after=[tt])
            out.free(e)
        return use

    w = d["w_mix_in"]
    project_tokens(k, w, 0, 512, lambda c: uT[:, c, :], use_q, ready=[u_ready])
    project_tokens(k, w, 512, 768, lambda c: uT[:, c, :], use_kv(2, False), tiles=NT,
                   more=(lambda c: ucT[:, c, :], CTX // P, use_kv(0, True)))

    PAD = 16
    pad, dbl = k.arena(2, S + 2 * PAD), k.arena(2, S + 2 * PAD)
    pooled = k.arena(2, S)
    k.dve(nc.vector.memset, pad, 0.0)
    k.dve(nc.vector.memset, dbl, 0.0)
    pooled_read = [None, None]
    pend = []

    def group_out(g, last):
        out = k.banks.take()
        t = k.mm(out.ap, grp[:, g, :], pooled[:, g % 2, :], after=[last, *out.wait])
        pooled_read[g % 2] = t
        e = k.act_fn(catT[:, 4 + g, :], out.ap, ACT.Copy, scale=p_scale[:, g:g + 1], after=[t])
        out.free(e)

    def use_p(g, bank, tok):
        x = pad[:, g % 2, :]
        k.dve(nc.vector.tensor_copy, x[:, PAD:PAD + S], bank.ap, after=[tok])
        n = S + 2 * PAD
        src = x
        for i in range(g + 1):
            dst = dbl[:, i % 2, :]
            step = 1 << i
            n -= step
            k.tt(dst[:, 0:n], src[:, 0:n], src[:, step:step + n], ALU.add)
            src = dst
        w2 = 1 << g
        k.tt(pooled[:, g % 2, :], src[:, PAD - w2:PAD - w2 + S], inv[:, g, :], ALU.mult, after=[pooled_read[g % 2]])
        last = k.tt(pooled[:, g % 2, :], pooled[:, g % 2, :], bank.ap, ALU.subtract)
        bank.free(last)
        if pend:
            group_out(*pend.pop())
        pend.append((g, last))

    project_features(k, w, 768, 1280, lambda c: uT[:, c, :], use_p)
    group_out(*pend.pop())
    k.barrier()

    k.arena.at = keep
    PT = k.arena(2, NK, S)
    prob = k.arena(2, 2, N_KEYS)
    stats = k.arena(2, 2, 2)
    k.prob_read = [None, None]
    pt_read = [None]

    def values(g):
        for i in range(2):
            head = g + 4 * i
            rows_ = slice(64 * (head % 2), 64 * (head % 2) + 64)
            out = k.banks.take()
            for kt in range(NK):
                t = k.mm(out.ap[rows_, :], v[:, kt, 64 * i:64 * i + 64], PT[:, i, kt, :], kt == 0, kt == NK - 1,
                         after=[*values.ready, *out.wait] if kt == 0 else ())
            e = k.evac(catT[rows_, head // 2, :], out.ap[rows_, :], after=[t])
            out.free(e)
        pt_read[0] = t
        return e

    for g in range(4):
        evs = []
        for t in range(NT):
            b = t % 2
            run = k.banks.take_run(4)
            for i in range(2):
                r = slice(64 * i, 64 * i + 64)
                for n0, n1 in ((0, 512), (512, N_KEYS)):
                    tok = k.mm(run.ap[:, 2 * i + n0 // 512, 0:n1 - n0], qT[r, g, t * P:(t + 1) * P], kT[r, n0:n1],
                               after=run.wait if n0 == 0 and i == 0 else ())
            sc = run.ap.rearrange("p (h b) n -> p h (b n)", h=2)[:, :, 0:N_KEYS]
            read, last = softmax_rows(k, sc, 2, N_KEYS, DH ** -0.5, prob[:, b], stats[:, b], after=[tok],
                                      out_free=[k.prob_read[b]])
            run.free(read)
            for i in range(2):
                for k0 in range(0, NK, 4):
                    n = min(4, NK - k0)
                    out = k.banks.take()
                    for j in range(n):
                        tok = k.tr(out.ap[:, j * P:(j + 1) * P], prob[:, b, i, (k0 + j) * P:(k0 + j + 1) * P],
                                   after=[last, *out.wait])
                    e = k.evac(PT[:, i, k0:k0 + n, t * P:(t + 1) * P],
                               out.ap[:, 0:n * P].rearrange("p (a b) -> p a b", a=n), after=[tok, pt_read[0]])
                    out.free(e)
                    evs.append(e)
            k.prob_read[b] = tok
        values.ready = evs[-4:]
        end = values(g)
    k.barrier()
    k.arena.at = top
    return catT



def short_conv(k, m):
    d, nc = k.dram, k.nc
    cols = m["cols"]
    yT = k.arena(NC, S)
    top = k.arena.at
    uT = k.arena(NC, S)
    taps = k.arena(3, NC)
    small = k.loads([(taps, d["conv_w_cols"])])
    ready = feature_major(k, k.h, uT, cols[:, 8:16, 0], cols[:, 0:8, 0])
    c_sb, z = k.arena(2, S), k.arena(2, S + 2)
    k.dve(nc.vector.memset, z, 0.0)
    w = d["w_conv_in"]
    for m0 in range(0, D, HALF):
        pieces = [k.weights(rows(w, 0, NC, part * D + m0, part * D + m0 + HALF)) for part in range(3)]
        for j in range(4):
            got = []
            for part in (1, 2, 0):
                bank, piece = k.banks.take(), pieces[part]
                for c in range(NC):
                    t = k.mm(bank.ap, piece.ap[:, c, j * P:(j + 1) * P], uT[:, c, :], c == 0, c == NC - 1,
                             after=[piece.landed, *bank.wait, ready] if c == 0 else ())
                if j == 3:
                    piece.done(t)
                got.append((bank, t))
            chunk, b = m0 // P + j, j % 2
            (cb, ct), (xb, xt), (bb, bt) = got
            a = k.act_fn(c_sb[:, b, :], cb.ap, ACT.Copy, after=[ct, short_conv.c_read[b]])
            cb.free(a)
            r = k.tt(z[:, b, 1:S + 1], c_sb[:, b, :], xb.ap, ALU.mult, after=[a, xt])
            short_conv.c_read[b] = r
            xb.free(r)
            y = yT[:, chunk, :]
            k.ts(y, z[:, b, 0:S], taps[:, 0, chunk:chunk + 1], None, ALU.mult, after=[small])
            k.stt(y, z[:, b, 1:S + 1], taps[:, 1, chunk:chunk + 1], y, ALU.mult, ALU.add)
            k.stt(y, z[:, b, 2:S + 2], taps[:, 2, chunk:chunk + 1], y, ALU.mult, ALU.add)
            last = k.tt(y, y, bb.ap, ALU.mult, after=[bt])
            bb.free(last)
    k.barrier()
    k.arena.at = top
    return yT



def experts(k, layer, m):
    d, nc = k.dram, k.nc
    cols = m["cols"]
    shift, scale = cols[:, 24:32, 0], cols[:, 32:40, 0]
    slotsT, out = k.arena(8, S), k.arena(8, D)
    top = k.arena.at
    uT = k.arena(NC, S)
    onehot = k.arena(NT, D)
    below = k.arena.at
    router = k.arena(NC, E)
    small = k.loads([(router, d["w_router"][layer].rearrange("(c p) e -> p c e", p=P))])
    ready = feature_major(k, k.h, uT, scale, shift)

    bank = k.banks.take()
    for t in range(NT):
        for c in range(NC):
            tok = k.mm(bank.ap[:, t * E:(t + 1) * E], uT[:, c, t * P:(t + 1) * P], router[:, c, :], c == 0, c == NC - 1,
                       after=[small, ready, *bank.wait] if t == c == 0 else ())
    logits = bank.ap[:, 0:NT * E].rearrange("p (t e) -> p t e", e=E)
    aff, mx = k.arena(NT, E), k.arena(NT)
    k.dve(nc.vector.tensor_reduce, mx, logits, AX, ALU.max, after=[tok])
    s = k.tt(aff, logits, mx.unsqueeze(2).to_broadcast([P, NT, E]), ALU.subtract)
    bank.free(s)
    a = k.act_fn(aff, aff, ACT.Exp, after=[s])
    k.dve(nc.vector.tensor_reduce, mx, aff, AX, ALU.add, after=[a])
    k.dve(nc.vector.reciprocal, mx, mx)
    s = k.tt(aff, aff, mx.unsqueeze(2).to_broadcast([P, NT, E]), ALU.mult)

    affT, work, best, ones = k.arena(S), k.arena(S), k.arena(8), k.arena(S)
    one = k.loads([(ones[0:E, :], d["ones"])])
    bank = k.banks.take()
    for t in range(NT):
        tok = k.tr(bank.ap[0:E, t * P:(t + 1) * P], aff[:, t, :], after=[s, *bank.wait])
    c0 = k.dve(nc.vector.tensor_copy, affT[0:E, :], bank.ap[0:E, :], after=[tok])
    bank.free(c0)
    src = affT
    for _ in range(CAP // 8):
        k.dve(nc.vector.max, best[0:E, :], src[0:E, :])
        k.dve(nc.vector.match_replace, work[0:E, :], best[0:E, :], src[0:E, :], -1.0)
        src = work
    k.ts(work[0:E, :], work[0:E, :], 0.0, None, ALU.is_lt)
    k.dve(nc.vector.tensor_tensor_scan, affT[0:E, :], ones[0:E, :], work[0:E, :], 0.0, ALU.mult, ALU.add, after=[one])
    s = k.tt(work[0:E, :], work[0:E, :], affT[0:E, :], ALU.mult)
    rank = k.arena(NT, E)
    bank = k.banks.take()
    for t in range(NT):
        tok = k.tr(bank.ap[:, t * E:(t + 1) * E], work[0:E, t * P:(t + 1) * P], after=[s, *bank.wait])
    c0 = k.dve(nc.vector.tensor_copy, rank, bank.ap[:, 0:NT * E].rearrange("p (t e) -> p t e", e=E), after=[tok])
    bank.free(c0)
    for t in range(NT):
        hot = k.tt(onehot[:, t, :].rearrange("p (e j) -> p e j", j=CAP),
                   k.slot_ids.unsqueeze(1).to_broadcast([P, E, CAP]),
                   rank[:, t, :].unsqueeze(2).to_broadcast([P, E, CAP]), ALU.is_equal)
    gated = k.arena(2, D)
    read = [None, None]
    slots_ready = []
    for t in range(NT):
        b = t % 2
        g = k.tt(gated[:, b, :].rearrange("p (e j) -> p e j", j=CAP),
                 onehot[:, t, :].rearrange("p (e j) -> p e j", j=CAP),
                 aff[:, t, :].unsqueeze(2).to_broadcast([P, E, CAP]), ALU.mult, after=[read[b]])
        for q in range(2):
            bank = k.banks.take()
            for i in range(4):
                tok = k.tr(bank.ap[:, i * P:(i + 1) * P], gated[:, b, (4 * q + i) * P:(4 * q + i + 1) * P],
                           after=[g, *bank.wait])
            e = k.evac(slotsT[:, 4 * q:4 * q + 4, t * P:(t + 1) * P],
                       bank.ap.rearrange("p (a b) -> p a b", a=4), after=[tok])
            bank.free(e)
            slots_ready.append(e)
        read[b] = tok
    k.barrier()

    k.arena.at = below
    xeT = uT
    act = k.arena(2, HALF)
    hid = k.arena(2, HALF)
    hidT = k.arena(2, 4, P)
    hid_read, hidT_read, act_read = [None, None], [None, None], [None, None]
    state = {}

    def gather(group):
        for c in range(NC):
            bank = k.banks.take()
            for t in range(NT):
                tok = k.mm(bank.ap, k.h[:, t, c * P:(c + 1) * P], onehot[:, t, group * HALF:(group + 1) * HALF],
                           t == 0, t == NT - 1, after=bank.wait if t == 0 else ())
            e = k.ts(xeT[:, c, :], bank.ap, scale[:, c:c + 1], shift[:, c:c + 1], ALU.mult, ALU.add, after=[tok])
            bank.free(e)
        state["gathered"] = e

    def up(e):
        got = []
        for w in ("w_exp_gate", "w_exp_up"):
            bank = k.banks.take()
            pieces = [k.weights(rows(d[w][layer, e], 4 * i, 4 * i + 4, 0, D)) for i in range(2)]
            for c in range(NC):
                piece = pieces[c // 4]
                x = xeT[:, c, (e % 8) * CAP:(e % 8 + 1) * CAP]
                for half in range(2):
                    t = k.mm(bank.ap[64 * half:64 * half + 64, :], x, piece.ap[:, c % 4, half * HALF:(half + 1) * HALF],
                             c == 0, c == NC - 1,
                             after=[piece.landed, state["gathered"], *bank.wait] if c % 4 == 0 and half == 0 else ())
                if c % 4 == 3:
                    piece.done(t)
            got.append((bank, t))
        (gb, gt), (ub, ut) = got
        b = e % 2
        a = k.act_fn(act[:, b, :], gb.ap, ACT.Silu, after=[gt, act_read[b]])
        gb.free(a)
        h = k.tt(hid[:, b, :], act[:, b, :], ub.ap, ALU.mult, after=[a, ut, hid_read[b]])
        act_read[b] = h
        ub.free(h)
        return h

    def down(e, h):
        b = e % 2
        bank = k.banks.take()
        for i in range(4):
            tok = k.tr(bank.ap[:, i * P:(i + 1) * P], hid[:, b, i * P:(i + 1) * P], after=[h, *bank.wait])
        hid_read[b] = tok
        v = k.evac(hidT[:, b], bank.ap.rearrange("p (a b) -> p a b", a=4), after=[tok, hidT_read[b]])
        bank.free(v)
        bank = k.banks.take()
        pieces = [k.weights(rows(d["w_exp_down"][layer, e], 4 * i, 4 * i + 4, 0, D)) for i in range(2)]
        for c in range(NC):
            piece = pieces[c // 4]
            x = hidT[:, b, c % 4, 64 * (c // 4):64 * (c // 4) + 64]
            for half in range(2):
                t = k.mm(bank.ap[64 * half:64 * half + 64, :], x, piece.ap[:, c % 4, half * HALF:(half + 1) * HALF],
                         c == 0, c == NC - 1, after=[piece.landed, v, *bank.wait] if c % 4 == 0 and half == 0 else ())
            if c % 4 == 3:
                piece.done(t)
        hidT_read[b] = t
        q = slice(64 * (e % 2), 64 * (e % 2) + 64)
        for half in range(2):
            s = k.evac(out[q, e // 2, half * HALF:(half + 1) * HALF], bank.ap[64 * half:64 * half + 64, :], after=[t])
            bank.free(s)

    before = None
    for e in range(E):
        if e % 8 == 0:
            gather(e // 8)
        h = up(e)
        if before is not None:
            down(*before)
        before = (e, h)
    down(*before)
    k.barrier()
    k.arena.at = top
    return slotsT, out


def scatter(k, slotsT, out, use):
    for t in range(NT):
        for half in range(2):
            bank = k.banks.take()
            for pair in range(E // 2):
                tok = k.mm(bank.ap, slotsT[:, pair, t * P:(t + 1) * P], out[:, pair, half * HALF:(half + 1) * HALF],
                           pair == 0, pair == E // 2 - 1, after=bank.wait if pair == 0 else ())
            use(t, half, bank, tok)



def add_residual(k):
    def use(t, half, bank, tok):
        hv = k.h[:, t, half * HALF:(half + 1) * HALF]
        bank.free(k.tt(hv, bank.ap, hv, ALU.add, after=[tok]))
    return use


def rms_scaled(k, dst, r, sq):
    for t in range(NT):
        a = k.act_fn(sq, k.h[:, t, :], ACT.Square, accum_out=r[:, t:t + 1],
                     after=[k.dve.last] if t == 0 else ())
    inverse_root(k, r, r, 1.0 / D, after=[a])
    for t in range(NT):
        last = k.ts(dst[:, t, :], k.h[:, t, :], r[:, t:t + 1], None, ALU.mult)
    return last


def normed(k, gain_cols, dst):
    mark = k.arena.at
    scaled, r, sq, gain = k.arena(NT, D), k.arena(NT), k.arena(D), k.arena(NC)
    small = k.loads([(gain, gain_cols)])
    last = rms_scaled(k, scaled, r, sq)
    ready = feature_major(k, scaled, dst, gain, None, ready=[last, small])
    k.barrier()
    k.arena.at = mark
    return ready


def swiglu(k, layer):
    d = k.dram
    mark = k.arena.at
    xT, hid, act = k.arena(NC, S), k.arena(NF, S), k.arena(2, S)
    ready = normed(k, d["ffn_norm_2_cols"][layer], xT)
    w1, w3, w2 = d["ffn_w1_2"][layer], d["ffn_w3_2"][layer], d["ffn_w2_2"][layer]
    act_read = [None, None]
    for m0 in range(0, FF, HALF):
        m1 = min(m0 + HALF, FF)
        pieces = [k.weights(rows(w, 0, NC, m0, m1)) for w in (w1, w3)]
        for j in range((m1 - m0) // P):
            got = []
            for piece in pieces:
                bank = k.banks.take()
                for c in range(NC):
                    t = k.mm(bank.ap, piece.ap[:, c, j * P:(j + 1) * P], xT[:, c, :], c == 0, c == NC - 1,
                             after=[piece.landed, ready, *bank.wait] if c == 0 else ())
                if (j + 1) * P == m1 - m0:
                    piece.done(t)
                got.append((bank, t))
            (gb, gt), (ub, ut) = got
            b = j % 2
            a = k.act_fn(act[:, b, :], gb.ap, ACT.Silu, after=[gt, act_read[b]])
            gb.free(a)
            h = k.tt(hid[:, m0 // P + j, :], act[:, b, :], ub.ap, ALU.mult, after=[a, ut])
            act_read[b] = h
            ub.free(h)
    use = add_residual(k)
    for half in range(2):
        banks = [k.banks.take() for _ in range(NT)]
        for c0 in range(0, NF, NC):
            c1 = min(c0 + NC, NF)
            piece = k.weights(rows(w2, c0, c1, half * HALF, (half + 1) * HALF))
            for t in range(NT):
                for c in range(c0, c1):
                    tok = k.mm(banks[t].ap, hid[:, c, t * P:(t + 1) * P], piece.ap[:, c - c0, :], c == 0, c == NF - 1,
                               after=[piece.landed, h, *(banks[t].wait if c == 0 else ())] if c == c0 else ())
                if c1 == NF:
                    use(t, half, banks[t], tok)
            piece.done(tok)
    k.barrier()
    k.arena.at = mark


def log1p_small(k, out, x, s, tmp):
    k.ts(tmp, x, 2.0, None, ALU.add)
    k.dve(k.nc.vector.reciprocal, tmp, tmp)
    k.tt(s, x, tmp, ALU.mult)
    k.tt(tmp, s, s, ALU.mult)
    k.ts(out, tmp, 1.0 / 17, 1.0 / 15, ALU.mult, ALU.add)
    for n in (13, 11, 9, 7, 5, 3, 1):
        k.tt(out, out, tmp, ALU.mult)
        k.ts(out, out, 1.0 / n, None, ALU.add)
    k.tt(out, out, s, ALU.mult)
    return k.ts(out, out, 2.0, None, ALU.mult)


def recurrent_retention(k):
    d, nc = k.dram, k.nc
    catT = k.arena(NC, S)
    top = k.arena.at
    xT = k.arena(NC, S)
    ready = normed(k, d["attn_norm_2_cols"][0], xT)
    x_of = lambda c: xT[:, c, :]
    w = d["ab_w_in_2"]
    qT, kT, v, gate = k.arena(4, S), k.arena(4, S), k.arena(NT, HALF), k.arena(NT, HALF)
    keep = k.arena.at

    yT, xr, conv = k.arena(4, S), k.arena(4, S + 4), k.arena(4, S)
    taps, bias, ga_b, gx_b, lam = k.arena(4, 4), k.arena(4), k.arena(4), k.arena(4), k.arena(4)
    ga, gx = k.arena(4, DH), k.arena(4, DH)
    small = k.loads([(bias, d["conv_b_2_cols"]), (ga_b, d["gate_a_b_2_cols"]), (gx_b, d["gate_x_b_2_cols"]),
                     (lam, d["lru_lambda_2_cols"]),
                     (taps, d["conv_w_2_cols"]),
                     *[(g[64 * p:64 * p + 64], d[n].rearrange("(c two) i j -> two i c j", two=2)[p])
                       for g, n in ((ga, "gate_a_w_2"), (gx, "gate_x_w_2")) for p in range(2)]])
    k.dve(nc.vector.memset, xr, 0.0)

    def use_y(j, bank, tok):
        bank.free(k.act_fn(yT[:, j, :], bank.ap, ACT.Gelu_apprx_tanh, after=[tok]))

    def use_x(j, bank, tok):
        bank.free(k.dve(nc.vector.tensor_copy, xr[:, j, 3:3 + S], bank.ap, after=[tok]))
        c = conv[:, j, :]
        k.ts(c, xr[:, j, 0:S], taps[:, 0, j:j + 1], bias[:, j:j + 1], ALU.mult, ALU.add, after=[small])
        for i in range(1, 4):
            t = k.stt(c, xr[:, j, i:i + S], taps[:, i, j:j + 1], c, ALU.mult, ALU.add)
        use_x.last = t

    project_features(k, w, 0, 512, x_of, use_y, ready=[ready])
    project_features(k, w, 512, 1024, x_of, use_x)

    neg, ex, rate, s1, s2 = (k.arena(4) for _ in range(5))
    k.ts(neg, lam, -1.0, None, ALU.mult)
    v0 = k.tt(ex, neg, lam, ALU.min)
    a = k.act_fn(ex, ex, ACT.Exp, after=[v0])
    k.ts(neg, neg, 0.0, None, ALU.max, after=[a])
    log1p_small(k, rate, ex, s1, s2)
    k.tt(rate, rate, neg, ALU.add)
    k.ts(rate, rate, 8.0, None, ALU.mult)
    nrate = s1
    k.ts(nrate, rate, -1.0, None, ALU.mult)

    r, i_, a_, u = k.arena(2, S), k.arena(2, S), k.arena(2, S), k.arena(2, S)
    for j in range(4):
        b = j % 2
        got = []
        for g, gb, dst in ((ga, ga_b, r), (gx, gx_b, i_)):
            bank = k.banks.take()
            for p in range(2):
                q = slice(64 * p, 64 * p + 64)
                t = k.mm(bank.ap[q, :], g[q, j, :], conv[q, j, :], after=[use_x.last, small, *bank.wait])
            a = k.act_fn(dst[:, b, :], bank.ap, ACT.Sigmoid, bias=gb[:, j:j + 1],
                         after=[t, recurrent_retention.read[b]])
            bank.free(a)
        a = k.act_fn(a_[:, b, :], r[:, b, :], ACT.Exp, scale=nrate[:, j:j + 1], after=[k.dve.last])
        a = k.act_fn(r[:, b, :], r[:, b, :], ACT.Tanh, scale=rate[:, j:j + 1])
        k.tt(u[:, b, :], a_[:, b, :], a_[:, b, :], ALU.mult, after=[a])
        v1 = k.stt(u[:, b, :], u[:, b, :], 1.0, r[:, b, :], ALU.add, ALU.mult)
        a = k.act_fn(r[:, b, :], u[:, b, :], ACT.Sqrt, after=[v1])
        k.tt(i_[:, b, :], i_[:, b, :], conv[:, j, :], ALU.mult, after=[a])
        k.tt(u[:, b, :], r[:, b, :], i_[:, b, :], ALU.mult)
        k.dve(nc.vector.tensor_tensor_scan, i_[:, b, :], a_[:, b, :], u[:, b, :], 0.0, ALU.mult, ALU.add)
        recurrent_retention.read[b] = k.tt(catT[:, j, :], i_[:, b, :], yT[:, j, :], ALU.mult)
    k.barrier()
    k.arena.at = keep

    cos, sin = k.arena(NT, 32), k.arena(NT, 32)
    rot, half = k.arena(HALF), k.arena(2, HALF // 2)
    small = k.loads([(cos, d["ret_cos"]), (sin, d["ret_sin"])])
    read = [None]

    def use_qk(dst, scale):
        def use(t, bank, tok):
            x = bank.ap.rearrange("p (h d) -> p h d", d=DH)
            o = rot.rearrange("p (h d) -> p h d", d=DH)
            last = rotate(k, x[:, :, 0:32], x[:, :, 32:64], o[:, :, 0:32], o[:, :, 32:64], cos[:, t, :], sin[:, t, :],
                          [half[:, i, :] for i in range(2)], (P, 8, 32), after=[tok, small, read[0]])
            bank.free(last)
            if scale is not None:
                last = k.ts(rot, rot, scale, None, ALU.mult)
            out = k.banks.take()
            for j in range(4):
                tt = k.tr(out.ap[:, j * P:(j + 1) * P], rot[:, j * P:(j + 1) * P], after=[last, *out.wait])
            read[0] = tt
            e = k.evac(dst[:, :, t * P:(t + 1) * P], out.ap.rearrange("p (g q) -> p g q", g=4), after=[tt])
            out.free(e)
        return use

    project_tokens(k, w, 1024, 1536, x_of, use_qk(qT, None))
    project_tokens(k, w, 1536, 2048, x_of, use_qk(kT, DH ** -0.5))
    project_tokens(k, w, 2048, 2560, x_of,
                   lambda t, bank, tok: bank.free(k.evac(v[:, t, :], bank.ap, after=[tok])))
    project_tokens(k, w, 2560, 3072, x_of,
                   lambda t, bank, tok: bank.free(k.act_fn(gate[:, t, :], bank.ap, ACT.Silu, after=[tok])))
    k.barrier()

    o = k.arena(NT, HALF)
    sT = k.arena(2, 4, S)
    o_read = [None, None]
    decay = k.weights(d["decay"])
    for head in range(8):
        q = slice(64 * (head % 2), 64 * (head % 2) + 64)
        b = head % 2
        for kt in range(NT):
            n = S - kt * P
            bank = k.banks.take()
            t = k.mm(bank.ap[:, 0:n], kT[q, head // 2, kt * P:(kt + 1) * P], qT[q, head // 2, kt * P:S], after=bank.wait)
            m_ = k.tt(sT[:, b, kt, 0:n], bank.ap[:, 0:n], decay.ap[:, head, 0:n], ALU.mult,
                      after=[t, decay.landed, o_read[b]])
            bank.free(m_)
        bank = k.banks.take()
        for t in range(NT):
            for kt in range(t + 1):
                tok = k.mm(bank.ap[:, t * DH:(t + 1) * DH], sT[:, b, kt, (t - kt) * P:(t - kt + 1) * P],
                           v[:, kt, head * DH:(head + 1) * DH], kt == 0, kt == t,
                           after=[m_, *bank.wait] if t == kt == 0 else ())
        o_read[b] = tok
        e = k.act_fn(o[:, :, head * DH:(head + 1) * DH], bank.ap[:, 0:NT * DH].rearrange("p (t d) -> p t d", d=DH),
                     ACT.Copy, after=[tok])
        bank.free(e)
    decay.done(m_)
    mu, var, sq = k.arena(NT, 8), k.arena(NT, 8), k.arena(HALF)
    for t in range(NT):
        x = o[:, t, :].rearrange("p (h d) -> p h d", d=DH)
        k.dve(nc.vector.tensor_reduce, mu[:, t, :], x, AX, ALU.add, after=[e])
        k.ts(mu[:, t, :], mu[:, t, :], 1.0 / DH, None, ALU.mult)
        k.tt(x, x, mu[:, t, :].unsqueeze(2).to_broadcast([P, 8, DH]), ALU.subtract)
        k.tt(sq, o[:, t, :], o[:, t, :], ALU.mult)
        k.dve(nc.vector.tensor_reduce, var[:, t, :], sq.rearrange("p (h d) -> p h d", d=DH), AX, ALU.add)
    inverse_root(k, var, var, 1.0 / DH)
    for t in range(NT):
        x = o[:, t, :].rearrange("p (h d) -> p h d", d=DH)
        k.tt(x, x, var[:, t, :].unsqueeze(2).to_broadcast([P, 8, DH]), ALU.mult)
        last = k.tt(o[:, t, :], o[:, t, :], gate[:, t, :], ALU.mult)
    for j in range(4):
        bank = k.banks.take()
        for t in range(NT):
            tok = k.tr(bank.ap[:, t * P:(t + 1) * P], o[:, t, j * P:(j + 1) * P], after=[last, *bank.wait])
        e = k.evac(catT[:, 4 + j, :], bank.ap, after=[tok])
        bank.free(e)
    k.barrier()
    k.arena.at = top
    return catT



def sparse_attention(k):
    d, nc = k.dram, k.nc
    oT = k.arena(NC, S)
    top = k.arena.at
    qT = k.arena(NC, S)
    ksT, kwT = k.arena(2, S), k.arena(2, S)
    vs, vw = k.arena(NT, 256), k.arena(NT, 256)
    kcT, vc = k.arena(2, N_CMP), k.arena(256)
    gates = k.arena(NT, 48)
    hide, seen = k.arena(NT, N_CMP), k.arena(NT, N_CMP)
    causal = k.arena(P)
    keep = k.arena.at
    xT = k.arena(NC, S)
    ready = normed(k, d["attn_norm_2_cols"][1], xT)
    x_of = lambda c: xT[:, c, :]
    cos, sin, ccos, csin = k.arena(NT, 8), k.arena(NT, 8), k.arena(8), k.arena(8)
    kc_in, vc_in = k.arena(2, S), k.arena(2, S)
    w1, w2, pe = [k.arena(32, DH) for _ in range(2)], [k.arena(DH) for _ in range(2)], [k.arena(32) for _ in range(2)]
    names = ("k", "v")
    pairs = [(cos, d["nsa_cos"]), (sin, d["nsa_sin"]), (ccos[0:N_CMP, :], d["cmp_cos"]), (csin[0:N_CMP, :], d["cmp_sin"]),
             (hide, d["cmp_hide"]), (seen, d["cmp_seen"]), (causal, d["causal"])]
    for i, n in enumerate(names):
        for p in range(2):
            q = slice(64 * p, 64 * p + 64)
            pairs += [(w1[i][q], d[f"cmp_{n}_w1_2"].rearrange("(l d) e -> d l e", d=DH)),
                      (w2[i][q], d[f"cmp_{n}_w2_2"]), (pe[i][q], d[f"cmp_pe_{n}_2_T"])]
    small = k.loads(pairs)
    w = d["nsa_w_in_2"]
    tm, half = k.arena(2, HALF), k.arena(2, 64)
    read = [None, None]
    turn = [0]

    def rotated(bank, tok, t, c0, c1, scale):
        b = turn[0] % 2
        turn[0] += 1
        n = (c1 - c0) // DH
        dst = tm[:, b, 0:c1 - c0]
        to, frm = dst, bank.ap[:, c0:c1]
        if n == 8:
            to = dst.rearrange("p (r g d) -> p g r d", g=2, r=4)
            frm = frm.rearrange("p (g r d) -> p g r d", g=2, r=4)
        a = k.act_fn(to, frm, ACT.Copy, scale=scale, after=[tok, read[b]])
        o = dst.rearrange("p (h d) -> p h d", d=DH)
        last = rotate(k, o[:, :, 0:8], o[:, :, 8:16], o[:, :, 0:8], o[:, :, 8:16], cos[:, t, :], sin[:, t, :],
                      [half[:, i, 0:8 * n] for i in range(2)], (P, n, 8), after=[a, small])
        return b, dst, a, last

    def use_q(a_):
        def use(t, bank, tok):
            b, dst, r, last = rotated(bank, tok, t, 0, HALF, DH ** -0.5)
            bank.free(r)
            out = k.banks.take()
            for g in range(4):
                tt = k.tr(out.ap[:, g * P:(g + 1) * P], dst[:, g * P:(g + 1) * P], after=[last, *out.wait])
            read[b] = tt
            e = k.evac(qT[:, 4 * a_:4 * a_ + 4, t * P:(t + 1) * P], out.ap.rearrange("p (g q) -> p g q", g=4), after=[tt])
            out.free(e)
        return use

    def use_kv(kdst, vdst):
        def use(t, bank, tok):
            b, dst, r, last = rotated(bank, tok, t, 0, 256, 1.0)
            r2 = k.act_fn(vdst[:, t, :], bank.ap[:, 256:512], ACT.Copy, after=[tok])
            bank.free(r2)
            out = k.banks.take()
            for g in range(2):
                tt = k.tr(out.ap[:, g * P:(g + 1) * P], dst[:, g * P:(g + 1) * P], after=[last, *out.wait])
            read[b] = tt
            e = k.evac(kdst[:, :, t * P:(t + 1) * P], out.ap[:, 0:2 * P].rearrange("p (g q) -> p g q", g=2), after=[tt])
            out.free(e)
        return use

    project_tokens(k, w, 0, 512, x_of, use_q(0), ready=[ready])
    project_tokens(k, w, 512, 1024, x_of, use_q(1))
    cmp_in = [kc_in[:, 0, :], kc_in[:, 1, :], vc_in[:, 0, :], vc_in[:, 1, :]]
    in_ready = []

    def use_cmp(j, bank, tok):
        e = k.evac(cmp_in[j], bank.ap, after=[tok])
        bank.free(e)
        in_ready.append(e)

    project_features(k, w, 1024, 1536, x_of, use_cmp)
    project_tokens(k, w, 1536, 2048, x_of, use_kv(ksT, vs))
    project_tokens(k, w, 2048, 2560, x_of, use_kv(kwT, vw))
    project_tokens(k, w, 2560, 2608, x_of,
                   lambda t, bank, tok: bank.free(k.act_fn(gates[:, t, :], bank.ap[:, 0:48], ACT.Sigmoid, after=[tok])))

    g_sb, bias = k.arena(2, 64), k.arena(2)
    cmp_tm = k.arena(256)
    for i, src in enumerate((kc_in, vc_in)):
        pe_bank = k.banks.take()
        for p in range(2):
            q = slice(64 * p, 64 * p + 64)
            for l in range(32):
                t = k.mm(pe_bank.ap[q, 0:1], w1[i][q, l, :], pe[i][q, l:l + 1], l == 0, l == 31,
                         after=[small, *pe_bank.wait] if l == 0 else ())
        v0 = k.dve(nc.vector.tensor_copy, bias[:, i:i + 1], pe_bank.ap[:, 0:1], after=[t])
        pe_bank.free(v0)
        bank = k.banks.take()
        for p in range(2):
            q = slice(64 * p, 64 * p + 64)
            for l in range(32):
                x = src[q, :, l:l + 16 * (N_CMP - 1) + 1:16]
                t = k.mm(bank.ap[q, 0:2 * N_CMP], w1[i][q, l, :], x, l == 0, l == 31,
                         after=[*in_ready, *bank.wait] if l == 0 else ())
        a = k.act_fn(g_sb[:, i, 0:2 * N_CMP], bank.ap[:, 0:2 * N_CMP], ACT.Gelu_apprx_tanh, bias=bias[:, i:i + 1], after=[t, v0])
        bank.free(a)
        dst = cmp_tm if i == 0 else vc
        for p in range(2):
            q = slice(64 * p, 64 * p + 64)
            bank2 = k.banks.take()
            for gp in range(2):
                t = k.mm(bank2.ap[0:N_CMP, gp * DH:(gp + 1) * DH], g_sb[q, i, gp * N_CMP:(gp + 1) * N_CMP], w2[i][q, :],
                         after=[a, *bank2.wait])
            c = k.dve(nc.vector.tensor_copy,
                      dst[0:N_CMP, :].rearrange("p (gp two d) -> p two gp d", two=2, d=DH)[:, p],
                      bank2.ap[0:N_CMP, 0:2 * DH].rearrange("p (gp d) -> p gp d", d=DH), after=[t])
            bank2.free(c)
        if i == 0:
            o = cmp_tm[0:N_CMP, :].rearrange("p (h d) -> p h d", d=DH)
            last = rotate(k, o[:, :, 0:8], o[:, :, 8:16], o[:, :, 0:8], o[:, :, 8:16], ccos[0:N_CMP, :], csin[0:N_CMP, :],
                          [half[0:N_CMP, j, 0:32] for j in range(2)], (N_CMP, 4, 8))
            out = k.banks.take()
            for gp in range(2):
                t = k.tr(out.ap[:, gp * N_CMP:(gp + 1) * N_CMP], cmp_tm[0:N_CMP, gp * P:(gp + 1) * P], after=[last, *out.wait])
            e = k.evac(kcT, out.ap[:, 0:2 * N_CMP].rearrange("p (g n) -> p g n", g=2), after=[t])
            out.free(e)
    k.barrier()
    k.arena.at = keep

    prob, stats = k.arena(2, 4, S), k.arena(2, 3, 4)
    PT = [[k.arena(4, P if branch == 0 else S) for branch in range(3)] for _ in range(2)]
    keys, vals = (kcT, ksT, kwT), (vc, vs, vw)
    prob_read, pt_read = [None, None], [None, None]
    g_of = [gates[:, t, :].rearrange("p (a g r b) -> p b a r g", a=2, g=2, b=3) for t in range(NT)]
    steps = [(a_, r0, t, branch) for a_ in range(2) for r0 in (0, 2) for t in range(NT) for branch in range(3)]

    def heads_of(a_, r0):
        return [8 * a_ + 4 * p + r0 + i for i in range(2) for p in range(2)]

    def scores(n):
        a_, r0, t, branch = steps[n]
        b, width = n % 2, N_CMP if branch == 0 else (t + 1) * P
        run = k.banks.take_run(4)
        for j in range(4):
            q = slice(64 * (j % 2), 64 * (j % 2) + 64)
            tok = k.mm(run.ap[:, j, 0:width], qT[q, 4 * a_ + r0 + j // 2, t * P:(t + 1) * P],
                       keys[branch][q, a_, 0:width], after=run.wait if j == 0 else ())
        sc = run.ap[:, :, 0:width]
        if branch == 0:
            k.tt(sc, sc, hide[:, t, :].unsqueeze(1).to_broadcast([P, 4, N_CMP]), ALU.add, after=[tok])
        else:
            diag = run.ap[:, :, width - P:width]
            k.tt(diag, diag, causal.unsqueeze(1).to_broadcast([P, 4, P]), ALU.add, after=[tok])
        gate = g_of[t][:, branch, a_, r0:r0 + 2, :]
        rd, last = softmax_rows(k, sc, 4, width, 1.0, prob[:, b], stats[:, b], gate=gate, after=[tok],
                                out_free=[prob_read[b]], keep=seen[:, t, :] if branch == 0 else None)
        run.free(rd)
        return last

    def transposes(n, last):
        a_, r0, t, branch = steps[n]
        b, tb = n % 2, (n // 3) % 2
        for j in range(4):
            out = k.banks.take()
            if branch == 0:
                tok = k.tr(out.ap[0:N_CMP, 0:P], prob[:, b, j, 0:N_CMP], after=[last, *out.wait])
                e = k.evac(PT[tb][0][0:N_CMP, j, :], out.ap[0:N_CMP, 0:P], after=[tok, pt_read[tb]])
            else:
                for kt in range(t + 1):
                    tok = k.tr(out.ap[:, kt * P:(kt + 1) * P], prob[:, b, j, kt * P:(kt + 1) * P],
                               after=[last, *out.wait])
                e = k.evac(PT[tb][branch][:, j, 0:(t + 1) * P], out.ap[:, 0:(t + 1) * P], after=[tok, pt_read[tb]])
            out.free(e)
        prob_read[b] = tok

    def values(n, ready):
        a_, r0, t, _ = steps[n]
        tb = (n // 3) % 2
        out = k.banks.take()
        first = [*ready, *out.wait]
        for j, head in enumerate(heads_of(a_, r0)):
            p, i = j % 2, j // 2
            o = out.ap[64 * i:64 * i + 64, p * P:(p + 1) * P]
            gc = slice((2 * a_ + p) * DH, (2 * a_ + p + 1) * DH)
            k.mm(o, vc[0:N_CMP, gc], PT[tb][0][0:N_CMP, j, :], True, False, after=first)
            first = ()
            for branch in (1, 2):
                for kt in range(t + 1):
                    tok = k.mm(o, vals[branch][:, kt, gc], PT[tb][branch][:, j, kt * P:(kt + 1) * P],
                               False, branch == 2 and kt == t)
        pt_read[tb] = tok
        c0 = 4 * a_ + r0 // 2
        e = k.evac(oT[:, c0:c0 + 3:2, t * P:(t + 1) * P], out.ap[:, 0:2 * P].rearrange("p (c q) -> p c q", c=2), after=[tok])
        out.free(e)

    last, due = None, None
    for n in range(len(steps)):
        now = scores(n)
        if due is not None:
            values(*due)
            due = None
        if n:
            transposes(n - 1, last)
            if n % 3 == 0:
                due = (n - 1, [k.dve.last, k.act.last])
        last = now
    transposes(len(steps) - 1, last)
    values(len(steps) - 1, [k.dve.last, k.act.last])
    k.barrier()
    k.arena.at = top
    return oT


def finish(k):
    nc = k.nc
    for line in (k.pe, k.dve, k.act, k.pool, k.sync):
        line.number()
    with nc.Block() as block:
        @block.sync
        def _(eng):
            k.sync.emit(eng)
            eng.wait_ge(k.out_count[0], k.out_count[1])

        @block.tensor
        def _(eng):
            k.pe.emit(eng)

        @block.vector
        def _(eng):
            k.dve.emit(eng)

        @block.scalar
        def _(eng):
            k.act.emit(eng)

        @block.gpsimd
        def _(eng):
            k.pool.emit(eng)



def build(nc, dram, out):
    with ExitStack() as ctx:
        k = Core(nc, ctx, dram)
        d = dram
        first = k.loads([(k.ident, d["ident"]), (k.sum_rows, d["sum_rows"]), (k.slot_ids, d["slot_ids"]),
                 (k.sum_cols, d["sum_cols"])])
        h_landed = k.loads([(k.h[:, :, :], d["x"][0].rearrange("(t p) n -> p t n", p=P))])

        k.startup = [first, h_landed]
        m = dict(cols=k.arena(48, 2), gates=k.arena(2, D))
        base = k.arena.at
        short_conv.c_read = [None, None]
        recurrent_retention.read = [None, None]
        for layer in range(2):
            m.update(part=k.arena(2, HALF), bias_cols=k.arena(48), gate_bias=k.arena(2, D))
            cond, raw = k.arena(NC, 32), k.arena(2, NC)
            small = k.loads([(raw[:, 0, :], d["c_cols"][0]), (raw[:, 1, :], d["c_ctx_cols"])])
            z = k.dve(nc.vector.memset, cond, 0.0)
            for i in range(2):
                k.cond_ready = k.act_fn(cond[:, :, i], raw[:, i, :], ACT.Silu, after=[z, small, *k.startup])
            modulation(k, layer, cond, m)
            k.barrier()
            k.arena.at = base
            w_out = d["w_mix_out"] if layer == 0 else d["w_conv_out"]
            mixT = attn_pool(k, m) if layer == 0 else short_conv(k, m)
            gain, bias = k.arena(D), k.arena(D)
            ready = k.loads([(gain, d["ln_mix_g"][layer, :].partition_broadcast(P)),
                             (bias, d["ln_mix_b"][layer, :].partition_broadcast(P))])
            use, _ = post_norm(k, m["gates"][:, 0, :], gain, bias, ready)
            project_out(k, w_out, lambda c: mixT[:, c, :], use)
            k.barrier()
            k.arena.at = base
            slotsT, ye = experts(k, layer, m)
            gain, bias = k.arena(D), k.arena(D)
            ready = k.loads([(gain, d["ln_ffn_g"][layer, :].partition_broadcast(P)),
                             (bias, d["ln_ffn_b"][layer, :].partition_broadcast(P))])
            use, _ = post_norm(k, m["gates"][:, 1, :], gain, bias, ready)
            scatter(k, slotsT, ye, use)
            k.barrier()
            k.arena.at = base

        k.arena.at = 0
        catT = recurrent_retention(k)
        project_out(k, d["ab_w_out_2"], lambda c: catT[:, c, :], add_residual(k))
        k.barrier()
        k.arena.at = 0
        swiglu(k, 0)
        oT = sparse_attention(k)
        project_out(k, d["nsa_w_out_2"], lambda c: oT[:, c, :], add_residual(k))
        k.barrier()
        k.arena.at = 0
        swiglu(k, 1)

        scaled, r, sq, gain = k.arena(NT, D), k.arena(NT), k.arena(D), k.arena(D)
        small = k.loads([(gain, d["final_norm_2"].partition_broadcast(P))])
        rms_scaled(k, scaled, r, sq)
        for t in range(NT):
            last = k.tt(scaled[:, t, :], scaled[:, t, :], gain, ALU.mult, after=[small])
            stored = k.sync.dma(nc.sync.dma_start, out[0, t * P:(t + 1) * P, :], scaled[:, t, :], k.out_count, after=[last])

        finish(k)



def feature_columns(v):
    return np.swapaxes(v.reshape(*v.shape[:-1], -1, P), -1, -2)


def kernel(**inputs):
    import concourse.bacc as bacc
    from concourse.bass_utils import run_bass_kernel_spmd

    a = {n: np.asarray(v) for n, v in inputs.items()}
    a["xT"] = np.ascontiguousarray(a["x"][0].T)
    a["ctxT"] = np.ascontiguousarray(a.pop("ctx")[0].T)
    for name in ("w_mix_in", "q_norm_g", "k_norm_g", "w_pool_grp", "pool_scale", "w_mix_out", "w_conv_in", "conv_w",
                 "w_conv_out", "ab_w_in_2", "conv_w_2", "conv_b_2", "gate_a_w_2", "gate_a_b_2", "gate_x_w_2",
                 "gate_x_b_2", "lru_lambda_2", "ab_w_out_2", "nsa_w_in_2", "cmp_pe_k_2", "cmp_k_w1_2", "cmp_k_w2_2",
                 "cmp_pe_v_2", "cmp_v_w1_2", "cmp_v_w2_2", "nsa_w_out_2"):
        a[name] = a[name][0]
    for name in ("c", "c_ctx", "b_mod", "pool_scale", "attn_norm_2", "ffn_norm_2", "conv_b_2", "gate_a_b_2",
                 "gate_x_b_2", "lru_lambda_2"):
        a[name + "_cols"] = feature_columns(a[name])
    for name in ("conv_w", "conv_w_2"):
        a[name + "_cols"] = feature_columns(a.pop(name)).transpose(1, 0, 2)
    for name in ("cmp_pe_k_2", "cmp_pe_v_2"):
        a[name + "_T"] = a.pop(name).T
    for name in ("c", "c_ctx", "pool_scale", "attn_norm_2", "ffn_norm_2", "conv_b_2", "gate_a_b_2", "gate_x_b_2",
                 "lru_lambda_2"):
        a.pop(name)
    a.update(shape_constants())
    nc = bacc.Bacc("TRN2", target_bir_lowering=False, num_devices=1)
    arrays, dram = {}, {}
    for name, v in a.items():
        v = np.ascontiguousarray(v)
        arrays[f"in_{name}"] = v
        dram[name] = nc.dram_tensor(f"in_{name}", v.shape, F32, kind="ExternalInput").ap()
    out = nc.dram_tensor("out", (1, S, D), F32, kind="ExternalOutput").ap()
    build(nc, dram, out)
    r = run_bass_kernel_spmd(nc, [arrays], core_ids=[0])
    return r.results[0]["out"]
```

```python
from contextlib import ExitStack

import numpy as np

import concourse.bass as bass
from concourse import mybir

F32 = mybir.dt.float32
ALU = mybir.AluOpType
ACT = mybir.ActivationFunctionType
AX = mybir.AxisListType.X

P = 128
D = 1024
S = 512
NT = S // P
NC = D // P
CTX = 256
DH = 64
E = 16
CAP = 2 * S // E
FF = ((8 * D // 3 + 255) // 256) * 256
NF = FF // P
EPS = 1e-6
ALPHA = 4.0 ** 0.25
NEG = -1e30
N_CMP = (S - 32) // 16 + 1
HALF = 512
SLOT = 4096
N_SLOTS = 3
MORE_SLOTS = 2
UNIT = SLOT // 2
F32R = mybir.dt.float32r



class Token:

    def __init__(self, line):
        self.line, self.named, self.value = line, False, 0

    def point(self):
        return self.line.sem, self.value


class Landed:

    def __init__(self, sem, value):
        self.sem, self.value = sem, value

    def point(self):
        return self.sem, self.value


class Line:

    def __init__(self, sem, chained):
        self.sem, self.chained, self.items, self.last = sem, chained, [], None
        self.fence = []

    def waits_once(self, after):
        self.fence = self.fence + list(after)

    def waits(self, after):
        after = [t for t in after if t is not None] + self.fence
        self.fence = []
        return after

    def __call__(self, issue, *args, after=(), **kw):
        after = self.waits(after)
        if self.chained and self.last is not None:
            after.append(self.last)
        for t in after:
            if isinstance(t, Token):
                t.named = True
        done = Token(self)
        self.items.append((after, issue, args, kw, done))
        self.last = done
        return done

    def dma(self, issue, out, in_, count, after=()):
        after = self.waits(after)
        for t in after:
            if isinstance(t, Token):
                t.named = True
        count[1] += 16
        done = Landed(count[0], count[1])
        self.items.append((after, issue, (out, in_), {}, done))
        return done

    def number(self):
        n = 0
        for *_, done in self.items:
            if isinstance(done, Token) and done.named:
                n += 1
                done.value = n

    def emit(self, eng):
        reached = {}
        for after, issue, args, kw, done in self.items:
            need = {}
            for t in after:
                sem, value = t.point()
                if value > need.get(id(sem), (sem, 0))[1]:
                    need[id(sem)] = (sem, value)
            for key, (sem, value) in need.items():
                if reached.get(key, 0) < value:
                    eng.wait_ge(sem, value)
                    reached[key] = value
            ins = issue(*args, **kw)
            if isinstance(done, Landed):
                ins.then_inc(done.sem, 16)
            elif done.named:
                ins.then_inc(self.sem, 1)


class Bank:
    def __init__(self, ap):
        self.ap, self.readers = ap, []

    def free(self, token):
        self.readers.append(token)


class Banks:

    def __init__(self, ap, banks=None):
        self.ap = ap
        self.banks = banks or [Bank(ap[:, i, :]) for i in range(8)]
        self.at = 0

    def part(self, i0, i1):
        return Banks(self.ap[:, i0:i1, :], self.banks[i0:i1])

    def take(self):
        b = self.banks[self.at % len(self.banks)]
        self.at += 1
        b.wait, b.readers = b.readers, []
        return b

    def take_run(self, n):
        while self.at % n:
            self.at += 1
        got = [self.take() for _ in range(n)]
        i = (self.at - n) % len(self.banks)
        run = Bank(self.ap[:, i:i + n, :])
        run.wait = [t for b in got for t in b.wait]

        def free(token):
            for b in got:
                b.free(token)
        run.free = free
        return run


class Arena:

    def __init__(self, nc, offset, words):
        self.nc, self.offset, self.words, self.at, self.made = nc, offset, words, 0, 0

    def place(self, at, shape, dtype=F32):
        n = int(np.prod(shape))
        self.made += 1
        v = self.nc.alloc_sbuf_tensor_at(f"scratch{self.made}", [P, n], dtype, offset=self.offset + 4 * at)[:, :]
        if len(shape) == 2:
            v = v.rearrange("p (a b) -> p a b", a=shape[0])
        elif len(shape) == 3:
            v = v.rearrange("p (a b c) -> p a b c", a=shape[0], b=shape[1])
        return v

    def __call__(self, *shape, dtype=F32):
        n = int(np.prod(shape))
        assert self.at + n <= self.words, (self.at, n, self.words)
        v = self.place(self.at, shape, dtype)
        self.at += -(-n // 8) * 8
        return v

    def r(self, *shape):
        return self(*shape, dtype=F32R)

    def parts(self, *shape):
        return self.r(*shape), self.r(*shape)


class Piece:
    def __init__(self, ap, landed, slot):
        self.ap, self.landed, self.slot = ap, landed, slot

    def done(self, token):
        self.slot["readers"] = [token]


def shape_constants():
    f = np.float32
    tok = np.arange(S)

    def rope(pos, inv):
        ang = pos.astype(f)[:, None] * inv.astype(f)
        return np.cos(ang).astype(f), np.sin(ang).astype(f)

    def tiles(a):
        return np.ascontiguousarray(a.reshape(-1, P, a.shape[1]).transpose(1, 0, 2))

    c = {}
    c["ident"] = np.eye(P, dtype=f)
    sum_cols = np.zeros((P, 2), f)
    for g in range(4):
        sum_cols[32 * g, 0] = sum_cols[32 * g + 1, 1] = 1
    c["sum_cols"] = sum_cols
    c["slot_ids"] = np.broadcast_to(np.arange(1, CAP + 1, dtype=f), (P, CAP)).copy()
    c["ones"] = np.ones((E, S), f)
    q = np.arange(P)
    c["causal"] = np.where(q[None, :] <= q[:, None], 0, NEG).astype(f)
    ends = np.arange(N_CMP) * 16 + 31
    seen = (ends[None, :] <= tok[:, None])
    c["cmp_seen"] = tiles(seen.astype(f))
    c["cmp_hide"] = tiles(np.where(seen, 0, NEG).astype(f))
    inv = f(10000.0) ** (-np.arange(0, 32, 2, dtype=f) / f(32))
    row_c, row_s = rope(tok // 64, inv)
    col_c, col_s = rope(tok % 64, inv)
    c["ax_cos"], c["ax_sin"] = tiles(np.concatenate([row_c, col_c], 1)), tiles(np.concatenate([row_s, col_s], 1))
    a, b = rope(tok, f(10000.0) ** (-np.arange(0, 64, 2, dtype=f) / f(64)))
    c["ret_cos"], c["ret_sin"] = tiles(a), tiles(b)
    inv = f(500000.0) ** (-np.arange(0, 16, 2, dtype=f) / f(16))
    a, b = rope(tok, inv)
    c["nsa_cos"], c["nsa_sin"] = tiles(a), tiles(b)
    c["cmp_cos"], c["cmp_sin"] = rope(ends, inv)
    counts = np.stack([np.minimum(tok + w // 2, S) - np.maximum(tok - w // 2, 0) for w in (2, 4, 8, 16)])
    c["pool_inv"] = np.broadcast_to((1.0 / counts).astype(f), (P, 4, S)).copy()
    log_g = np.log1p(-(2.0 ** (-5.0 - np.arange(8))))
    diff = np.arange(S)[None, :] - np.arange(P)[:, None]
    dec = np.where(diff[None] >= 0, np.exp(np.maximum(diff, 0)[None] * log_g[:, None, None]), 0.0)
    c["decay"] = np.ascontiguousarray(dec.transpose(1, 0, 2)).astype(f)
    return c



class Core:

    def __init__(self, nc, ctx, dram):
        self.nc, self.dram = nc, dram

        def sem(name):
            return ctx.enter_context(nc.semaphore(name))

        def sbuf(name, shape):
            return ctx.enter_context(nc.sbuf_tensor(name, shape, F32))

        self.pe = Line(sem("pe_done"), chained=False)
        self.dve = Line(sem("dve_done"), chained=True)
        self.act = Line(sem("act_done"), chained=True)
        self.pool = Line(sem("pool_done"), chained=True)
        self.sync = Line(sem("sync_done"), chained=False)
        self.banks = Banks(ctx.enter_context(nc.psum_tensor("psum", [P, 8, HALF], F32))[:, :, :])
        ring = sbuf("weight_ring", [P, N_SLOTS, SLOT])
        self.base_slots = [dict(ap=ring[:, i, :], count=[sem(f"slot{i}_landed"), 0], readers=[])
                           for i in range(N_SLOTS)]
        self.slots, self.next_slot = list(self.base_slots), 0
        self.new_sem, self.n_loads = sem, 0
        self.h = sbuf("h", [P, NT, D])
        self.consts = sbuf("consts", [P, 2 * P + CAP + 2])
        self.ident = self.consts[:, 0:P]
        self.ones = self.consts[:, P:2 * P]
        self.slot_ids = self.consts[:, 2 * P:2 * P + CAP]
        self.sum_cols = self.consts[:, 2 * P + CAP:2 * P + CAP + 2]
        words = (nc.sbuf_bytes_remaining - 256) // 256 * 64
        sbuf("rest", [P, words])
        low = words - 4 * UNIT
        self.arena = Arena(nc, nc.sbuf_base - 4 * words, low)
        place = self.arena.place
        self.unit_region = low
        self.unit_bufs = [dict(hi=place(low + 2 * i * UNIT, [UNIT], F32R),
                               lo=place(low + (2 * i + 1) * UNIT, [UNIT], F32R), readers=[]) for i in range(2)]
        self.next_unit = 0
        self.more_slots = [dict(ap=place(low + i * SLOT, [SLOT]), count=[sem(f"more_slot{i}_landed"), 0],
                                readers=[]) for i in range(MORE_SLOTS)]
        self.flip = 0
        self.out_count = [sem("out_landed"), 0]

    def widen_ring(self):
        for slot in self.more_slots:
            slot["readers"] = [t for u in self.unit_bufs for t in u["readers"]] + [
                t for t in (self.pe.last, self.act.last, self.dve.last) if t is not None]
        self.slots += self.more_slots

    def narrow_ring(self):
        for u in self.unit_bufs:
            u["readers"] = [t for slot in self.more_slots for t in slot["readers"]]
        self.slots = [s for s in self.slots if all(s is not m for m in self.more_slots)]

    def weights(self, src):
        chunks, cols = src.shape[1], src.shape[2]
        slot = self.slots.pop(0)
        self.slots.append(slot)
        assert slot["readers"] is not None and chunks * cols <= SLOT
        view = slot["ap"][:, 0:chunks * cols].rearrange("p (c n) -> p c n", c=chunks)
        landed = self.sync.dma(self.nc.sync.dma_start, view, src, slot["count"], after=slot["readers"])
        slot["readers"] = None
        return Piece(view, landed, slot)

    def loads(self, pairs, after=()):
        count = [self.new_sem(f"load{self.n_loads}_landed"), 0]
        self.n_loads += 1
        self.pool.waits_once(after)
        for out, in_ in pairs:
            t = self.pool.dma(self.nc.gpsimd.dma_start, out, in_, count)
        return t

    def barrier(self):
        lines = [self.pe, self.dve, self.act, self.pool]
        for line in lines:
            line.fence = line.fence + [o.last for o in lines if o.last is not None and (o is not line or o is self.pool)]

    def mm3(self, out, lhsT, rhs, start=True, stop=True, after=()):
        (lh, ll), (rh, rl) = lhsT, rhs
        self.mm(out, lh, rh, start, False, after=after)
        self.mm(out, lh, rl, False, False)
        return self.mm(out, ll, rh, False, stop)

    def split(self, hi, lo, src, after=()):
        a = self.act_fn(hi, src, ACT.Copy, after=after)
        return self.tt(lo, src, hi.bitcast(F32), ALU.subtract, after=[a, *after])

    def units(self, plan):
        last_of = {key: i for i, (key, _, _) in enumerate(plan)}
        pieces, made = {}, {}

        def make(i):
            key, src, take = plan[i]
            if key not in pieces:
                pieces[key] = self.weights(src)
            piece = pieces[key]
            view = take(piece.ap)
            n = view.shape[1] * view.shape[2]
            buf = self.unit_bufs[self.next_unit % 2]
            self.next_unit += 1
            hi, lo = (buf[x][:, 0:n].rearrange("p (c n) -> p c n", c=view.shape[1]) for x in ("hi", "lo"))
            ready = self.split(hi, lo, view, after=[piece.landed, *buf["readers"]])
            if last_of[key] == i:
                piece.done(ready)

            def done(token):
                buf["readers"] = [token]
            made[i] = (hi, lo, ready, done)

        make(0)
        for i in range(len(plan)):
            if i + 1 < len(plan):
                make(i + 1)
            yield made.pop(i)

    def mm(self, out, lhsT, rhs, start=True, stop=True, after=()):
        return self.pe(self.nc.tensor.matmul, out, lhsT, rhs, start=start, stop=stop, after=after)

    def tr(self, out, in_, after=()):
        k = in_.shape[0]
        return self.pe(self.nc.tensor.transpose, out, in_, self.ident[0:k, 0:k], after=after)

    def tt(self, out, a, b, op, after=()):
        return self.dve(self.nc.vector.tensor_tensor, out, a, b, op, after=after)

    def ts(self, out, a, s1, s2, op0, op1=None, after=()):
        if op1 is None:
            return self.dve(self.nc.vector.tensor_scalar, out, a, s1, None, op0, after=after)
        return self.dve(self.nc.vector.tensor_scalar, out, a, s1, s2, op0, op1, after=after)

    def stt(self, out, a, s, b, op0, op1, after=()):
        return self.dve(self.nc.vector.scalar_tensor_tensor, out, a, s, b, op0, op1, after=after)

    def act_fn(self, out, in_, fn, after=(), **kw):
        return self.act(self.nc.scalar.activation, out, in_, fn, after=after, **kw)

    def evac(self, out, in_, after=()):
        self.flip ^= 1
        if self.flip:
            return self.act_fn(out, in_, ACT.Copy, after=after)
        return self.dve(self.nc.vector.tensor_copy, out, in_, after=after)



def rows(w, c0, c1, n0, n1):
    return w[c0 * P:c1 * P, n0:n1].rearrange("(c p) n -> p c n", p=P)


def column_units(name, w, n0, n1):
    plan = []
    for m0 in range(n0, n1, HALF):
        m1 = min(m0 + HALF, n1)
        for u0 in range(0, m1 - m0, 256):
            u1 = min(u0 + 256, m1 - m0)
            plan.append(((name, m0), rows(w, 0, NC, m0, m1), lambda v, u0=u0, u1=u1: v[:, :, u0:u1]))
    return plan


def chunk_units(name, w, c0, c1, n0, n1):
    plan = []
    for p0 in range(c0, c1, 8):
        p1 = min(p0 + 8, c1)
        for u0 in range(0, p1 - p0, 4):
            u1 = min(u0 + 4, p1 - p0)
            plan.append(((name, p0, n0), rows(w, p0, p1, n0, n1), lambda v, u0=u0, u1=u1: v[:, u0:u1, :]))
    return plan


def feature_products(k, unit, x, use, ready):
    hi, lo, split, done = unit
    for i in range(hi.shape[2] // P):
        bank = k.banks.take()
        s = slice(i * P, (i + 1) * P)
        for c in range(NC):
            t = k.mm3(bank.ap[:, 0:S], (hi[:, c, s], lo[:, c, s]), (x[0][:, c, :], x[1][:, c, :]), c == 0, c == NC - 1,
                      after=[split, *bank.wait, *ready] if c == 0 else ())
        if (i + 1) * P >= hi.shape[2]:
            done(t)
        use(i, bank, t)


def project_features(k, w, n0, n1, x, use, ready=()):
    for n, unit in enumerate(k.units(column_units("w", w, n0, n1))):
        feature_products(k, unit, x, lambda i, bank, t: use(2 * n + i, bank, t), ready)


def token_products(k, units, tiles, use, ready, width, total):
    banks = [k.banks.take() for _ in tiles]
    c0 = 0
    for hi, lo, split, done in units:
        n = hi.shape[1]
        for t, x in enumerate(tiles):
            for c in range(c0, c0 + n):
                tok = k.mm3(banks[t].ap[:, 0:width], x(c), (hi[:, c - c0, :], lo[:, c - c0, :]), c == 0, c == total - 1,
                            after=[split, *ready, *(banks[t].wait if c == 0 else ())] if c == c0 else ())
            if t == len(tiles) - 1:
                done(tok)
            if c0 + n == total:
                use(t, banks[t], tok)
        c0 += n


def tile_parts(x, t):
    s = slice(t * P, (t + 1) * P)
    return lambda c: (x[0][:, c, s], x[1][:, c, s])


def project_tokens(k, w, n0, n1, x, use, ready=(), more=None):
    tiles = [tile_parts(x, t) for t in range(NT)]
    if more:
        tiles += [tile_parts(more[0], t) for t in range(more[1])]

    def both(t, bank, tok):
        use(t, bank, tok) if t < NT else more[2](t - NT, bank, tok)
    token_products(k, k.units(chunk_units("w", w, 0, NC, n0, n1)), tiles, both, ready, n1 - n0, NC)


def project_out(k, w, xT, use, ready=()):
    pieces = [k.weights(rows(w, 0, NC, half * HALF, (half + 1) * HALF)) for half in range(2)]
    for t in range(NT):
        for half, piece in enumerate(pieces):
            bank = k.banks.take()
            for c in range(NC):
                tok = k.mm(bank.ap, xT(c)[:, t * P:(t + 1) * P], piece.ap[:, c, :], c == 0, c == NC - 1,
                           after=[piece.landed, *bank.wait, *ready] if c == 0 else ())
            if t == NT - 1:
                piece.done(tok)
            use(t, half, bank, tok)


def feature_major(k, src, dst, scale, shift, ready=()):
    for c in range(NC):
        bank = k.banks.take()
        for t in range(NT):
            tok = k.tr(bank.ap[:, t * P:(t + 1) * P], src[:, t, c * P:(c + 1) * P],
                       after=[*bank.wait, *ready] if t == 0 else ())
        if shift is None:
            done = k.ts(dst[:, c, :], bank.ap, scale[:, c:c + 1], None, ALU.mult, after=[tok])
        else:
            done = k.ts(dst[:, c, :], bank.ap, scale[:, c:c + 1], shift[:, c:c + 1], ALU.mult, ALU.add, after=[tok])
        bank.free(done)
    return done


def feature_parts(k, src, dst, scale, shift, ready=()):
    tmp = k.arena(2, S) if shift is not None else None
    for c in range(NC):
        bank = k.banks.take()
        for t in range(NT):
            tok = k.tr(bank.ap[:, t * P:(t + 1) * P], src[:, t, c * P:(c + 1) * P],
                       after=[*bank.wait, *ready] if t == 0 else ())
        hi, lo = dst[0][:, c, :], dst[1][:, c, :]
        if shift is None:
            a = k.act_fn(hi, bank.ap, ACT.Copy, scale=scale[:, c:c + 1], after=[tok, *ready])
            done = k.stt(lo, bank.ap, scale[:, c:c + 1], hi.bitcast(F32), ALU.mult, ALU.subtract, after=[a])
            bank.free(done)
        else:
            v = tmp[:, c % 2, :]
            s = k.ts(v, bank.ap, scale[:, c:c + 1], shift[:, c:c + 1], ALU.mult, ALU.add, after=[tok])
            bank.free(s)
            done = k.split(hi, lo, v, after=[s])
    return done


def inverse_root(k, out, in_, scale, after=()):
    v = k.ts(out, in_, scale, EPS, ALU.mult, ALU.add, after=after)
    a = k.act_fn(out, out, ACT.Sqrt, after=[v])
    return k.dve(k.nc.vector.reciprocal, out, out, after=[a])



def modulation_steps(k, layer, m):
    cols, bias_cols, cond = m["cols"], m["bias_cols"], m["cond"]
    part = [m["part"][:, i, :] for i in range(2)]
    part_read = [None, None]
    small = k.loads([(bias_cols, k.dram["b_mod_cols"][layer])])
    pieces = 6 * D // HALF
    made = {}

    def add_partials(j):
        buf, tok = made.pop(j)
        bank = k.banks.take()
        for i in range(4):
            t = k.mm(bank.ap[:, 2 * i:2 * i + 2], part[buf][:, i * P:(i + 1) * P], k.sum_cols,
                     after=[tok, *bank.wait] if i == 0 else ())
        part_read[buf] = t
        done = k.tt(cols[:, 4 * j:4 * j + 4, :], bank.ap[:, 0:8].rearrange("p (a b) -> p a b", b=2),
                    bias_cols[:, 4 * j:4 * j + 4].unsqueeze(2).to_broadcast([P, 4, 2]), ALU.add,
                    after=[t, small])
        bank.free(done)
        return done

    for j in range(pieces):
        piece = k.weights(rows(k.dram["w_mod"][layer], 0, NC, j * HALF, (j + 1) * HALF))
        bank = k.banks.take()
        for r in range(2):
            for g in range(4):
                c = 4 * r + g
                t = k.mm(bank.ap[32 * g:32 * g + 32, :], cond[:, c, :], piece.ap[:, c, :], r == 0, r == 1,
                         after=[piece.landed, k.cond_ready, *bank.wait] if c == 0 else ())
        piece.done(t)
        buf = j % 2
        done = k.act_fn(part[buf], bank.ap, ACT.Copy, after=[t, part_read[buf]])
        bank.free(done)
        made[j] = (buf, done)
        if j:
            add_partials(j - 1)
        yield
    add_partials(pieces - 1)
    k.ts(cols[:, 8:16, :], cols[:, 8:16, :], 1.0, None, ALU.add)
    m["ready"] = k.ts(cols[:, 32:40, :], cols[:, 32:40, :], 1.0, None, ALU.add)
    yield


def spread(k, col):
    row, diag, ready = k.arena(D), k.arena(NC, P), []
    for c in range(NC):
        v = k.ts(diag[:, c, :], k.ident, col[:, c:c + 1], None, ALU.mult)
    for half in range(2):
        bank = k.banks.take()
        for i in range(4):
            t = k.mm(bank.ap[:, i * P:(i + 1) * P], k.ones, diag[:, 4 * half + i, :], after=[v, *bank.wait])
        e = k.evac(row[:, half * HALF:(half + 1) * HALF], bank.ap, after=[t])
        bank.free(e)
        ready.append(e)
    return row, ready


def post_norm(k, gate, gain, bias, spread_done, ready):
    z = k.arena(2, D)
    st = k.arena(2, 2, 6)
    mv = k.arena(2, 2)
    r = k.arena(2, 1)
    out_read = [None, None]

    def use(t, half, bank, tok):
        b = t % 2
        zb = z[:, b, half * HALF:(half + 1) * HALF]
        done = k.tt(zb, bank.ap, gate[:, half * HALF:(half + 1) * HALF], ALU.mult,
                    after=[tok, *spread_done, out_read[b]])
        bank.free(done)
        k.stt(zb, k.h[:, t, half * HALF:(half + 1) * HALF], ALPHA, zb, ALU.mult, ALU.add)
        k.dve(k.nc.vector.bn_stats, st[:, b, half, :], zb)
        if half:
            k.dve(k.nc.vector.bn_aggr, mv[:, b, :], st[:, b, :, :])
            inverse_root(k, r[:, b, :], mv[:, b, 1:2], 1.0)
            shift = k.stt(mv[:, b, 1:2], mv[:, b, 0:1], -1.0, r[:, b, :], ALU.mult, ALU.mult)
            a = k.act_fn(z[:, b, :], z[:, b, :], ACT.Identity, scale=r[:, b, :], bias=mv[:, b, 1:2], after=[shift])
            v = k.tt(z[:, b, :], z[:, b, :], gain, ALU.mult, after=[a, *ready])
            out_read[b] = k.pool(k.nc.gpsimd.tensor_tensor, k.h[:, t, :], z[:, b, :], bias, ALU.add, after=[v])
    return use



def head_norm(k, src, heads, gain, tmp, small, out, after):
    sq = tmp[:, 0:heads * DH]
    a = k.act_fn(sq, src, ACT.Square, after=after)
    k.dve(k.nc.vector.tensor_reduce, small[:, 0:heads], sq.rearrange("p (h d) -> p h d", d=DH), AX, ALU.add, after=[a])
    inverse_root(k, small[:, 0:heads], small[:, 0:heads], 1.0 / DH)
    o = out.rearrange("p (h d) -> p h d", d=DH)
    if heads == 8:
        for kv in range(2):
            hs = slice(4 * kv, 4 * kv + 4)
            t = k.tt(out.rearrange("p (g kv d) -> p g kv d", g=4, kv=2)[:, :, kv, :],
                     src.rearrange("p (h d) -> p h d", d=DH)[:, hs, :],
                     small[:, hs].unsqueeze(2).to_broadcast([P, 4, DH]), ALU.mult)
    else:
        t = k.tt(o, src.rearrange("p (h d) -> p h d", d=DH), small[:, 0:heads].unsqueeze(2).to_broadcast([P, heads, DH]),
                 ALU.mult)
    last = k.tt(o, o, gain.unsqueeze(1).to_broadcast([P, heads, DH]), ALU.mult)
    return t, last


def rotate(k, x0, x1, out0, out1, cos, sin, tmp, shape, after=()):
    n, heads, half = shape
    c = cos.unsqueeze(1).to_broadcast([n, heads, half])
    s = sin.unsqueeze(1).to_broadcast([n, heads, half])
    a, b = [x.rearrange("p (h d) -> p h d", h=heads) for x in tmp]
    k.tt(a, x0, c, ALU.mult, after=after)
    k.tt(b, x1, s, ALU.mult)
    k.tt(a, a, b, ALU.subtract)
    k.tt(b, x0, s, ALU.mult)
    t = k.tt(out1, x1, c, ALU.mult)
    k.tt(out1, out1, b, ALU.add)
    return k.dve(k.nc.vector.tensor_copy, out0, a)


def exponentials(k, scores, n_heads, n, scale, out, stats, after=(), out_free=()):
    mx, sm = stats[:, 0], stats[:, 1]
    k.dve(k.nc.vector.tensor_reduce, mx, scores, AX, ALU.max, after=after)
    v = k.ts(mx, mx, -scale, None, ALU.mult)
    for i in range(n_heads):
        a = k.act_fn(out[:, i, 0:n], scores[:, i, :], ACT.Exp, bias=mx[:, i:i + 1], scale=scale,
                     accum_out=sm[:, i:i + 1], after=[v, *out_free])
    return a


def normalise(k, n_heads, n, out, stats, done, gate=None, keep=None):
    sm = stats[:, 1, 0:n_heads]
    k.dve(k.nc.vector.reciprocal, sm, sm, after=[done])
    if gate is not None:
        k.tt(sm.rearrange("p (r g) -> p r g", g=2), sm.rearrange("p (r g) -> p r g", g=2), gate, ALU.mult)
    for i in range(n_heads):
        if keep is not None:
            last = k.stt(out[:, i, 0:n], out[:, i, 0:n], sm[:, i:i + 1], keep, ALU.mult, ALU.mult)
        else:
            last = k.ts(out[:, i, 0:n], out[:, i, 0:n], sm[:, i:i + 1], None, ALU.mult)
    return last



def attn_pool(k, m, filler):
    d, nc = k.dram, k.nc
    cols = m["cols"]
    N_KEYS = CTX + S
    NK = N_KEYS // P
    catT = m["catT"]
    top = k.arena.at
    qT, kT, v = k.arena(4, S), k.arena(2, N_KEYS), k.arena(NK, P)
    heads_end = k.arena.at
    uT, ucT = k.arena.parts(NC, S), k.arena.parts(NC, CTX)
    keep = k.arena.at
    cos, sin = k.arena(NT, 32), k.arena(NT, 32)
    gq, gk = k.arena(DH), k.arena(DH)
    raw, raw_ctx = catT, m["raw_ctx"]
    landed = m["raw_landed"]
    small = k.loads([(cos, d["ax_cos"]), (sin, d["ax_sin"]),
                     (gq, d["q_norm_g"].partition_broadcast(P)), (gk, d["k_norm_g"].partition_broadcast(P))])
    for c in range(NC):
        for x, parts, i in ((raw, uT, 0), (raw_ctx, ucT, 1)):
            s = k.ts(x[:, c, :], x[:, c, :], cols[:, 8 + c, i:i + 1], cols[:, c, i:i + 1], ALU.mult, ALU.add,
                     after=[landed])
            u_ready = k.split(parts[0][:, c, :], parts[1][:, c, :], x[:, c, :], after=[s])

    for i in range(2):
        zeroed = k.dve(nc.vector.memset, kT[64 * (1 - i):64 * (1 - i) + 64, i, :], 0.0)
    tmp, st = k.arena(HALF), k.arena(8)
    qn, half = k.arena(HALF), k.arena(2, HALF // 2)
    rope_read = [None]

    def pairs(x):
        return x.rearrange("p (h d two) -> p h d two", two=2, d=DH // 2)

    def rope_tile(src, heads, gain, t, after):
        n = heads * DH
        read, last = head_norm(k, src, heads, gain, tmp, st, qn[:, 0:n], [*after, rope_read[0]])
        if t is not None:
            x = pairs(qn[:, 0:n])
            last = rotate(k, x[:, :, :, 0], x[:, :, :, 1], x[:, :, :, 0], x[:, :, :, 1], cos[:, t, :], sin[:, t, :],
                          [half[:, i, 0:n // 2] for i in range(2)], (P, heads, DH // 2))
        return read, last

    def use_q(t, bank, tok):
        read, last = rope_tile(bank.ap, 8, gq, t, [tok, small])
        bank.free(read)
        out = k.banks.take()
        for g in range(4):
            tt = k.tr(out.ap[:, g * P:(g + 1) * P], qn[:, g * P:(g + 1) * P], after=[last, *out.wait])
        rope_read[0] = tt
        e = k.evac(qT[:, :, t * P:(t + 1) * P], out.ap.rearrange("p (g q) -> p g q", g=4), after=[tt])
        out.free(e)

    def use_kv(first, is_ctx):
        def use(t, bank, tok):
            kt = first + t
            a = k.act_fn(v[:, kt, :], bank.ap[:, P:2 * P], ACT.Copy, after=[tok])
            read, last = rope_tile(bank.ap[:, 0:P], 2, gk, None if is_ctx else t, [tok, small])
            bank.free(read)
            bank.free(a)
            out = k.banks.take()
            tt = k.tr(out.ap[:, 0:P], qn[:, 0:P], after=[last, *out.wait])
            rope_read[0] = tt
            for i in range(2):
                q = slice(64 * i, 64 * i + 64)
                e = k.dve(nc.vector.tensor_copy, kT[q, i, kt * P:(kt + 1) * P], out.ap[q, 0:P], after=[tt])
            out.free(e)
        return use

    w = d["w_mix_in"]
    project_tokens(k, w, 0, 512, uT, use_q, ready=[u_ready])
    project_tokens(k, w, 512, 768, uT, use_kv(2, False), more=(ucT, CTX // P, use_kv(0, True)))
    k.barrier()
    k.arena.at = keep

    PAD = 16
    inv, grp, p_scale = k.arena(4, S), k.arena(4, P), k.arena(4)
    small = k.loads([(inv, d["pool_inv"]), (grp, d["w_pool_grp"].rearrange("g c d -> c g d")),
                     (p_scale, d["pool_scale_cols"])])
    pad, dbl = k.arena(2, S + 2 * PAD), k.arena(2, S + 2 * PAD)
    pooled = k.arena(2, S)
    k.dve(nc.vector.memset, pad, 0.0)
    k.dve(nc.vector.memset, dbl, 0.0)
    pooled_read = [None, None]
    pend = []

    def group_out(g, last):
        out = k.banks.take()
        t = k.mm(out.ap, grp[:, g, :], pooled[:, g % 2, :], after=[last, *out.wait])
        pooled_read[g % 2] = t
        e = k.act_fn(catT[:, 4 + g, :], out.ap, ACT.Copy, scale=p_scale[:, g:g + 1], after=[t])
        out.free(e)

    def use_p(g, bank, tok):
        x = pad[:, g % 2, :]
        k.dve(nc.vector.tensor_copy, x[:, PAD:PAD + S], bank.ap, after=[tok])
        n = S + 2 * PAD
        src = x
        for i in range(g + 1):
            dst = dbl[:, i % 2, :]
            step = 1 << i
            n -= step
            k.tt(dst[:, 0:n], src[:, 0:n], src[:, step:step + n], ALU.add)
            src = dst
        w2 = 1 << g
        k.tt(pooled[:, g % 2, :], src[:, PAD - w2:PAD - w2 + S], inv[:, g, :], ALU.mult, after=[pooled_read[g % 2], small])
        last = k.tt(pooled[:, g % 2, :], pooled[:, g % 2, :], bank.ap, ALU.subtract)
        bank.free(last)
        if pend:
            group_out(*pend.pop())
        pend.append((g, last))

    project_features(k, w, 768, 1280, uT, use_p)
    group_out(*pend.pop())
    k.barrier()

    k.arena.at = heads_end
    PT = k.arena(2, NK, S)
    prob = k.arena(2, 2, N_KEYS)
    stats = k.arena(2, 2, 2)
    prob_read, pt_read = [None, None], [None]
    steps = [(g, t) for g in range(4) for t in range(NT)]

    def scores(n):
        g, t = steps[n]
        made = []
        for i in range(2):
            run = score_banks.take_run(2)
            for n0, n1 in ((0, 512), (512, N_KEYS)):
                tok = k.mm(run.ap[:, n0 // 512, 0:n1 - n0], qT[:, g, t * P:(t + 1) * P], kT[:, i, n0:n1],
                           after=run.wait if n0 == 0 else ())
            made.append((run, tok))
        return made

    def exps(n, i, made):
        b = n % 2
        run, tok = made[i]
        sc = run.ap.rearrange("p b n -> p (b n)")[:, 0:N_KEYS].unsqueeze(1)
        done = exponentials(k, sc, 1, N_KEYS, DH ** -0.5, prob[:, b, i:i + 1], stats[:, b, :, i:i + 1],
                            after=[tok], out_free=[prob_read[b]])
        run.free(done)
        return done

    def transposes(n, i, last):
        g, t = steps[n]
        b = n % 2
        for k0 in range(0, NK, 4):
            w_ = min(4, NK - k0)
            out = k.banks.take()
            for j in range(w_):
                tok = k.tr(out.ap[:, j * P:(j + 1) * P], prob[:, b, i, (k0 + j) * P:(k0 + j + 1) * P],
                           after=[last, *out.wait])
            e = k.evac(PT[:, i, k0:k0 + w_, t * P:(t + 1) * P],
                       out.ap[:, 0:w_ * P].rearrange("p (a b) -> p a b", a=w_), after=[tok, pt_read[0]])
            out.free(e)
        if i:
            prob_read[b] = tok

    def values(g, ready):
        out = value_bank.take()
        for kt in range(NK):
            for i in range(2):
                t = k.mm(out.ap[64 * i:64 * i + 64, :], v[:, kt, 64 * i:64 * i + 64], PT[:, i, kt, :],
                         kt == 0, kt == NK - 1, after=[*ready, *out.wait] if kt == 0 else ())
        pt_read[0] = t
        return lambda: values_out(g, out, t)

    def values_out(g, out, t):
        for i in range(2):
            head = g + 4 * i
            e = k.evac(catT[64 * (head % 2):64 * (head % 2) + 64, head // 2, :], out.ap[64 * i:64 * i + 64, :], after=[t])
            out.free(e)

    all_banks = k.banks
    score_banks, k.banks, value_bank = all_banks.part(0, 4), all_banks.part(4, 7), all_banks.part(7, 8)
    done, due = None, None
    for n in range(len(steps) + 1):
        if n < len(steps):
            made = scores(n)
        evacuate = values(*due) if due else lambda: None
        due = None
        if n:
            last = normalise(k, 2, N_KEYS, prob[:, (n - 1) % 2], stats[:, (n - 1) % 2], done)
        for i in range(2):
            if n < len(steps):
                done = exps(n, i, made)
            if n:
                transposes(n - 1, i, last)
        evacuate()
        if n and n % NT == 0:
            due = (steps[n - 1][0], [k.dve.last, k.act.last])
        next(filler, None)
    values(*due)()
    for _ in filler:
        pass
    k.banks = all_banks
    k.barrier()
    k.arena.at = top
    return catT



def short_conv(k, m):
    d, nc = k.dram, k.nc
    cols = m["cols"]
    yT = k.arena(NC, S)
    top = k.arena.at
    uT = k.arena.parts(NC, S)
    taps = k.arena(3, NC)
    small = k.loads([(taps, d["conv_w_cols"])])
    ready = feature_parts(k, k.h, uT, cols[:, 8:16, 0], cols[:, 0:8, 0])
    c_sb, z = k.arena(2, S), k.arena(2, S + 2)
    c_read = [None, None]
    k.dve(nc.vector.memset, z, 0.0)
    w = d["w_conv_in"]
    plans = [column_units(part, w, part * D, (part + 1) * D) for part in (1, 2, 0)]
    got = []

    def take(i, bank, t):
        got.append((bank, t))

    for n, unit in enumerate(k.units([u for three in zip(*plans) for u in three])):
        feature_products(k, unit, uT, take, [ready])
        if n % 3 < 2:
            continue
        for j in range(2):
            (cb, ct), (xb, xt), (bb, bt) = got[j], got[2 + j], got[4 + j]
            chunk, b = 2 * (n // 3) + j, j
            a = k.act_fn(c_sb[:, b, :], cb.ap, ACT.Copy, after=[ct, c_read[b]])
            cb.free(a)
            r = k.tt(z[:, b, 1:S + 1], c_sb[:, b, :], xb.ap, ALU.mult, after=[a, xt])
            c_read[b] = r
            xb.free(r)
            y = yT[:, chunk, :]
            k.ts(y, z[:, b, 0:S], taps[:, 0, chunk:chunk + 1], None, ALU.mult, after=[small])
            k.stt(y, z[:, b, 1:S + 1], taps[:, 1, chunk:chunk + 1], y, ALU.mult, ALU.add)
            k.stt(y, z[:, b, 2:S + 2], taps[:, 2, chunk:chunk + 1], y, ALU.mult, ALU.add)
            last = k.tt(y, y, bb.ap, ALU.mult, after=[bt])
            bb.free(last)
        got.clear()
    k.barrier()
    k.arena.at = top
    return yT



def experts(k, layer, m):
    d, nc = k.dram, k.nc
    cols = m["cols"]
    shift, scale = cols[:, 24:32, 0], cols[:, 32:40, 0]
    k.widen_ring()
    slotsT, slot_gate = k.arena.r(8, S), k.arena(E)
    aff, rank = k.arena(NT, E), k.arena(NT, E)
    xeT = k.arena(NC, E * CAP)
    below = k.arena.at
    onehot = k.arena.r(NT, D)
    h_parts = k.arena.parts(NT, D)
    k.arena.at = below - NC * E * CAP
    uT = k.arena(NC, S)
    router = k.arena(NC, E)
    small = k.loads([(router, d["w_router"][layer].rearrange("(c p) e -> p c e", p=P))])
    ready = feature_major(k, k.h, uT, scale, shift)

    for t in range(NT):
        hi = h_parts[0][:, t, :]
        a = k.act_fn(hi, k.h[:, t, :], ACT.Copy)
        k.pool(nc.gpsimd.tensor_tensor, h_parts[1][:, t, :], k.h[:, t, :], hi.bitcast(F32), ALU.subtract, after=[a])

    bank = k.banks.take()
    for t in range(NT):
        for c in range(NC):
            tok = k.mm(bank.ap[:, t * E:(t + 1) * E], uT[:, c, t * P:(t + 1) * P], router[:, c, :], c == 0, c == NC - 1,
                       after=[small, ready, *bank.wait] if t == c == 0 else ())
    logits = bank.ap[:, 0:NT * E].rearrange("p (t e) -> p t e", e=E)
    mx = k.arena(NT)
    k.dve(nc.vector.tensor_reduce, mx, logits, AX, ALU.max, after=[tok])
    s = k.tt(aff, logits, mx.unsqueeze(2).to_broadcast([P, NT, E]), ALU.subtract)
    bank.free(s)
    a = k.act_fn(aff, aff, ACT.Exp, after=[s])
    k.dve(nc.vector.tensor_reduce, mx, aff, AX, ALU.add, after=[a])
    k.dve(nc.vector.reciprocal, mx, mx)
    s = k.tt(aff, aff, mx.unsqueeze(2).to_broadcast([P, NT, E]), ALU.mult)

    affT, work, best, ones = k.arena(S), k.arena(S), k.arena(8), k.arena(S)
    one = k.loads([(ones[0:E, :], d["ones"])])
    bank = k.banks.take()
    for t in range(NT):
        tok = k.tr(bank.ap[0:E, t * P:(t + 1) * P], aff[:, t, :], after=[s, *bank.wait])
    c0 = k.dve(nc.vector.tensor_copy, affT[0:E, :], bank.ap[0:E, :], after=[tok])
    bank.free(c0)
    src = affT
    for _ in range(CAP // 8):
        k.dve(nc.vector.max, best[0:E, :], src[0:E, :])
        k.dve(nc.vector.match_replace, work[0:E, :], best[0:E, :], src[0:E, :], -1.0)
        src = work
    k.ts(work[0:E, :], work[0:E, :], 0.0, None, ALU.is_lt)
    k.dve(nc.vector.tensor_tensor_scan, affT[0:E, :], ones[0:E, :], work[0:E, :], 0.0, ALU.mult, ALU.add, after=[one])
    s = k.tt(work[0:E, :], work[0:E, :], affT[0:E, :], ALU.mult)
    bank = k.banks.take()
    for t in range(NT):
        tok = k.tr(bank.ap[:, t * E:(t + 1) * E], work[0:E, t * P:(t + 1) * P], after=[s, *bank.wait])
    c0 = k.dve(nc.vector.tensor_copy, rank, bank.ap[:, 0:NT * E].rearrange("p (t e) -> p t e", e=E), after=[tok])
    bank.free(c0)
    for t in range(NT):
        k.tt(onehot[:, t, :].rearrange("p (e j) -> p e j", j=CAP),
             k.slot_ids.unsqueeze(1).to_broadcast([P, E, CAP]),
             rank[:, t, :].unsqueeze(2).to_broadcast([P, E, CAP]), ALU.is_equal)
    k.barrier()
    assert k.arena.at <= below
    k.arena.at = below

    for group in range(2):
        for c in range(NC):
            bank = k.banks.take()
            for t in range(NT):
                for part in h_parts:
                    tok = k.mm(bank.ap, part[:, t, c * P:(c + 1) * P], onehot[:, t, group * HALF:(group + 1) * HALF],
                               t == 0 and part is h_parts[0], t == NT - 1 and part is h_parts[1],
                               after=bank.wait if t == 0 and part is h_parts[0] else ())
            e = k.ts(xeT[:, c, group * HALF:(group + 1) * HALF], bank.ap, scale[:, c:c + 1], shift[:, c:c + 1],
                     ALU.mult, ALU.add, after=[tok])
            bank.free(e)
    bank = k.banks.take()
    for pair in range(E // 2):
        for t in range(NT):
            tok = k.mm(bank.ap[:, 2 * pair:2 * pair + 2], onehot[:, t, pair * P:(pair + 1) * P].bitcast(F32),
                       aff[:, t, 2 * pair:2 * pair + 2], t == 0, t == NT - 1,
                       after=bank.wait if pair == t == 0 else ())
    gathered = k.dve(nc.vector.tensor_copy, slot_gate, bank.ap[:, 0:E], after=[tok])
    bank.free(gathered)
    k.barrier()

    low = k.arena.r(8, D)
    high = k.arena.place(below - NC * E * CAP, (NC, E * CAP), F32R)
    top = k.arena.at
    act = k.arena(2, HALF)
    hid = k.arena(2, HALF)
    hidT = k.arena(2, 4, P)
    y, landed = k.arena(D), []
    hid_read, hidT_read, act_read = [None, None], [None, None], [None, None]

    def up(e):
        got = []
        for w in ("w_exp_gate", "w_exp_up"):
            bank = k.banks.take()
            pieces = [k.weights(rows(d[w][layer, e], 4 * i, 4 * i + 4, 0, D)) for i in range(2)]
            for c in range(NC):
                piece = pieces[c // 4]
                x = xeT[:, c, e * CAP:(e + 1) * CAP]
                for half in range(2):
                    t = k.mm(bank.ap[64 * half:64 * half + 64, :], x, piece.ap[:, c % 4, half * HALF:(half + 1) * HALF],
                             c == 0, c == NC - 1,
                             after=[piece.landed, gathered, *bank.wait] if c % 4 == 0 and half == 0 else ())
                if c % 4 == 3:
                    piece.done(t)
            got.append((bank, t))
        (gb, gt), (ub, ut) = got
        b = e % 2
        a = k.act_fn(act[:, b, :], gb.ap, ACT.Silu, after=[gt, act_read[b]])
        gb.free(a)
        h = k.tt(hid[:, b, :], act[:, b, :], ub.ap, ALU.mult, after=[a, ut, hid_read[b]])
        act_read[b] = h
        ub.free(h)
        return h

    def down(e, h):
        b = e % 2
        bank = k.banks.take()
        for i in range(4):
            tok = k.tr(bank.ap[:, i * P:(i + 1) * P], hid[:, b, i * P:(i + 1) * P], after=[h, *bank.wait])
        hid_read[b] = tok
        v = k.evac(hidT[:, b], bank.ap.rearrange("p (a b) -> p a b", a=4), after=[tok, hidT_read[b]])
        bank.free(v)
        bank = k.banks.take()
        pieces = [k.weights(rows(d["w_exp_down"][layer, e], 4 * i, 4 * i + 4, 0, D)) for i in range(2)]
        for c in range(NC):
            piece = pieces[c // 4]
            x = hidT[:, b, c % 4, 64 * (c // 4):64 * (c // 4) + 64]
            for half in range(2):
                t = k.mm(bank.ap[64 * half:64 * half + 64, :], x, piece.ap[:, c % 4, half * HALF:(half + 1) * HALF],
                         c == 0, c == NC - 1, after=[piece.landed, v, *bank.wait] if c % 4 == 0 and half == 0 else ())
            if c % 4 == 3:
                piece.done(t)
        hidT_read[b] = t
        q = slice(64 * (e % 2), 64 * (e % 2) + 64)
        for half in range(2):
            s = k.evac(y[q, half * HALF:(half + 1) * HALF], bank.ap[64 * half:64 * half + 64, :], after=[t])
            bank.free(s)
            landed.append(s)
        pair, gate = e // 2, slot_gate[q, e:e + 1]
        hi = high[q, :, pair * P:(pair + 1) * P]
        lo, yc = [x.rearrange("p (c n) -> p c n", c=NC) for x in (low[q, pair, :], y[q, :])]
        a = k.act_fn(hi, yc, ACT.Copy, scale=gate, after=landed[-2:])
        k.stt(lo, yc, gate, hi.bitcast(F32), ALU.mult, ALU.subtract, after=[a])

    onehot_t = k.arena(2, D)
    onehot_read = [None, None]

    def transposed_slots(t):
        b = t % 2
        g = k.tt(onehot_t[:, b, :].rearrange("p (e j) -> p e j", j=CAP),
                 k.slot_ids.unsqueeze(1).to_broadcast([P, E, CAP]),
                 rank[:, t, :].unsqueeze(2).to_broadcast([P, E, CAP]), ALU.is_equal, after=[onehot_read[b]])
        for q in range(2):
            bank = k.banks.take()
            for i in range(4):
                tok = k.tr(bank.ap[:, i * P:(i + 1) * P], onehot_t[:, b, (4 * q + i) * P:(4 * q + i + 1) * P],
                           after=[g, *bank.wait])
            e = k.evac(slotsT[:, 4 * q:4 * q + 4, t * P:(t + 1) * P],
                       bank.ap.rearrange("p (a b) -> p a b", a=4), after=[tok])
            bank.free(e)
        onehot_read[b] = tok

    before = None
    for e in range(E):
        if 2 <= e < 2 + NT:
            transposed_slots(e - 2)
        h = up(e)
        if before is not None:
            down(*before)
        before = (e, h)
    down(*before)
    k.narrow_ring()
    k.barrier()
    k.arena.at = top
    return slotsT, (high, low)


def scatter(k, slotsT, out, use):
    high, low = out
    for t in range(NT):
        for half in range(2):
            bank = k.banks.take()
            for pair in range(E // 2):
                for part in (high[:, 4 * half:4 * half + 4, pair * P:(pair + 1) * P],
                             low[:, pair, half * HALF:(half + 1) * HALF]):
                    first = pair == 0 and part.shape[1] == 4
                    tok = k.mm(bank.ap, slotsT[:, pair, t * P:(t + 1) * P], part, first,
                               pair == E // 2 - 1 and part.shape[1] != 4, after=bank.wait if first else ())
            use(t, half, bank, tok)



def add_residual(k):
    def use(t, half, bank, tok):
        hv = k.h[:, t, half * HALF:(half + 1) * HALF]
        bank.free(k.tt(hv, bank.ap, hv, ALU.add, after=[tok]))
    return use


def rms_scaled(k, dst, r):
    for t in range(NT):
        a = k.act_fn(dst[:, t, :], k.h[:, t, :], ACT.Square, accum_out=r[:, t:t + 1],
                     after=[k.dve.last] if t == 0 else ())
    inverse_root(k, r, r, 1.0 / D, after=[a])
    for t in range(NT):
        last = k.ts(dst[:, t, :], k.h[:, t, :], r[:, t:t + 1], None, ALU.mult)
    return last


def normed(k, gain_cols, dst):
    mark = k.arena.at
    scaled, r, gain = k.arena(NT, D), k.arena(NT), k.arena(NC)
    small = k.loads([(gain, gain_cols)])
    last = rms_scaled(k, scaled, r)
    ready = feature_parts(k, scaled, dst, gain, None, ready=[last, small])
    k.barrier()
    k.arena.at = mark
    return ready


def swiglu(k, layer):
    d = k.dram
    mark = k.arena.at
    x = k.arena.parts(NC, S)
    ready = normed(k, d["ffn_norm_2_cols"][layer], x)
    w1, w3, w2 = d["ffn_w1_2"][layer], d["ffn_w3_2"][layer], d["ffn_w2_2"][layer]
    GROUP = 12
    hid = k.arena.parts(GROUP, S)
    act, prod = k.arena(2, S), k.arena(2, S)
    act_read, prod_read = [None, None], [None, None]
    use = add_residual(k)
    hid_read = None
    for f0 in range(0, NF, GROUP):
        f1 = min(f0 + GROUP, NF)
        plans = [column_units(name, w, f0 * P, f1 * P) for name, w in (("w1", w1), ("w3", w3))]
        got = []
        for n, unit in enumerate(k.units([u for two in zip(*plans) for u in two])):
            feature_products(k, unit, x, lambda i, bank, t: got.append((bank, t)), [ready])
            if n % 2 == 0:
                continue
            for b in range(2):
                (gb, gt), (ub, ut) = got[b], got[2 + b]
                j = n // 2 * 2 + b
                a = k.act_fn(act[:, b, :], gb.ap, ACT.Silu, after=[gt, act_read[b]])
                gb.free(a)
                h = k.tt(prod[:, b, :], act[:, b, :], ub.ap, ALU.mult, after=[a, ut, prod_read[b]])
                act_read[b] = h
                ub.free(h)
                made = k.split(hid[0][:, j, :], hid[1][:, j, :], prod[:, b, :], after=[h, hid_read])
                prod_read[b] = made
            got.clear()
        for half in range(2):
            token_products(k, k.units(chunk_units("w2", w2, f0, f1, half * HALF, (half + 1) * HALF)),
                           [tile_parts(hid, t) for t in range(NT)],
                           lambda t, bank, tok: use(t, half, bank, tok), [made], HALF, f1 - f0)
        hid_read = k.pe.last
    k.barrier()
    k.arena.at = mark


def log1p_small(k, out, x, s, tmp):
    k.ts(tmp, x, 2.0, None, ALU.add)
    k.dve(k.nc.vector.reciprocal, tmp, tmp)
    k.tt(s, x, tmp, ALU.mult)
    k.tt(tmp, s, s, ALU.mult)
    k.ts(out, tmp, 1.0 / 17, 1.0 / 15, ALU.mult, ALU.add)
    for n in (13, 11, 9, 7, 5, 3, 1):
        k.tt(out, out, tmp, ALU.mult)
        k.ts(out, out, 1.0 / n, None, ALU.add)
    k.tt(out, out, s, ALU.mult)
    return k.ts(out, out, 2.0, None, ALU.mult)


def recurrent_retention(k):
    d, nc = k.dram, k.nc
    catT = k.arena(NC, S)
    top = k.arena.at
    x = k.arena.parts(NC, S)
    ready = normed(k, d["attn_norm_2_cols"][0], x)
    w = d["ab_w_in_2"]
    keep = k.arena.at

    yT, xr, conv = k.arena(4, S), k.arena(4, S + 4), k.arena(4, S)
    taps, bias, ga_b, gx_b, lam = k.arena(4, 4), k.arena(4), k.arena(4), k.arena(4), k.arena(4)
    ga, gx = k.arena(4, DH), k.arena(4, DH)
    small = k.loads([(bias, d["conv_b_2_cols"]), (ga_b, d["gate_a_b_2_cols"]), (gx_b, d["gate_x_b_2_cols"]),
                     (lam, d["lru_lambda_2_cols"]),
                     (taps, d["conv_w_2_cols"]),
                     *[(g[64 * p:64 * p + 64], d[n].rearrange("(c two) i j -> two i c j", two=2)[p])
                       for g, n in ((ga, "gate_a_w_2"), (gx, "gate_x_w_2")) for p in range(2)]])
    k.dve(nc.vector.memset, xr, 0.0)

    def use_y(j, bank, tok):
        bank.free(k.act_fn(yT[:, j, :], bank.ap, ACT.Gelu_apprx_tanh, after=[tok]))

    def use_x(j, bank, tok):
        bank.free(k.dve(nc.vector.tensor_copy, xr[:, j, 3:3 + S], bank.ap, after=[tok]))
        c = conv[:, j, :]
        k.ts(c, xr[:, j, 0:S], taps[:, 0, j:j + 1], bias[:, j:j + 1], ALU.mult, ALU.add, after=[small])
        for i in range(1, 4):
            t = k.stt(c, xr[:, j, i:i + S], taps[:, i, j:j + 1], c, ALU.mult, ALU.add)
        use_x.last = t

    project_features(k, w, 0, 512, x, use_y, ready=[ready])
    project_features(k, w, 512, 1024, x, use_x)

    neg, ex, rate, s1, s2 = (k.arena(4) for _ in range(5))
    k.ts(neg, lam, -1.0, None, ALU.mult)
    v0 = k.tt(ex, neg, lam, ALU.min)
    a = k.act_fn(ex, ex, ACT.Exp, after=[v0])
    k.ts(neg, neg, 0.0, None, ALU.max, after=[a])
    log1p_small(k, rate, ex, s1, s2)
    k.tt(rate, rate, neg, ALU.add)
    k.ts(rate, rate, 8.0, None, ALU.mult)
    nrate = s1
    k.ts(nrate, rate, -1.0, None, ALU.mult)

    lru_read = [None, None]
    r, i_, a_, u = k.arena(2, S), k.arena(2, S), k.arena(2, S), k.arena(2, S)
    for j in range(4):
        b = j % 2
        got = []
        for g, gb, dst in ((ga, ga_b, r), (gx, gx_b, i_)):
            bank = k.banks.take()
            for p in range(2):
                q = slice(64 * p, 64 * p + 64)
                t = k.mm(bank.ap[q, :], g[q, j, :], conv[q, j, :], after=[use_x.last, small, *bank.wait])
            a = k.act_fn(dst[:, b, :], bank.ap, ACT.Sigmoid, bias=gb[:, j:j + 1],
                         after=[t, lru_read[b]])
            bank.free(a)
        a = k.act_fn(a_[:, b, :], r[:, b, :], ACT.Exp, scale=nrate[:, j:j + 1], after=[k.dve.last])
        a = k.act_fn(r[:, b, :], r[:, b, :], ACT.Tanh, scale=rate[:, j:j + 1])
        k.tt(u[:, b, :], a_[:, b, :], a_[:, b, :], ALU.mult, after=[a])
        v1 = k.stt(u[:, b, :], u[:, b, :], 1.0, r[:, b, :], ALU.add, ALU.mult)
        a = k.act_fn(r[:, b, :], u[:, b, :], ACT.Sqrt, after=[v1])
        k.tt(i_[:, b, :], i_[:, b, :], conv[:, j, :], ALU.mult, after=[a])
        k.tt(u[:, b, :], r[:, b, :], i_[:, b, :], ALU.mult)
        k.dve(nc.vector.tensor_tensor_scan, i_[:, b, :], a_[:, b, :], u[:, b, :], 0.0, ALU.mult, ALU.add)
        lru_read[b] = k.tt(catT[:, j, :], i_[:, b, :], yT[:, j, :], ALU.mult)
    k.barrier()
    k.arena.at = keep

    qT, kT, v, gate = k.arena(4, S), k.arena(8, S), k.arena(NT, HALF), k.arena(NT, HALF)
    for i in range(2):
        k.dve(nc.vector.memset, kT[64 * (1 - i):64 * (1 - i) + 64, i:8:2, :], 0.0)
    cos, sin = k.arena(NT, 32), k.arena(NT, 32)
    rot, half = k.arena(HALF), k.arena(2, HALF // 2)
    small = k.loads([(cos, d["ret_cos"]), (sin, d["ret_sin"])])
    read = [None]

    def use_qk(dst, scale):
        def use(t, bank, tok):
            x = bank.ap.rearrange("p (h d) -> p h d", d=DH)
            o = rot.rearrange("p (h d) -> p h d", d=DH)
            last = rotate(k, x[:, :, 0:32], x[:, :, 32:64], o[:, :, 0:32], o[:, :, 32:64], cos[:, t, :], sin[:, t, :],
                          [half[:, i, :] for i in range(2)], (P, 8, 32), after=[tok, small, read[0]])
            bank.free(last)
            if scale is not None:
                last = k.ts(rot, rot, scale, None, ALU.mult)
            out = k.banks.take()
            for j in range(4):
                tt = k.tr(out.ap[:, j * P:(j + 1) * P], rot[:, j * P:(j + 1) * P], after=[last, *out.wait])
            read[0] = tt
            o4 = out.ap.rearrange("p (g q) -> p g q", g=4)
            if dst is qT:
                e = k.evac(dst[:, :, t * P:(t + 1) * P], o4, after=[tt])
            else:
                for i in range(2):
                    q = slice(64 * i, 64 * i + 64)
                    e = k.dve(nc.vector.tensor_copy, dst[q, i:8:2, t * P:(t + 1) * P], o4[q], after=[tt])
            out.free(e)
        return use

    project_tokens(k, w, 1024, 1536, x, use_qk(qT, None))
    project_tokens(k, w, 1536, 2048, x, use_qk(kT, DH ** -0.5))
    project_tokens(k, w, 2048, 2560, x,
                   lambda t, bank, tok: bank.free(k.evac(v[:, t, :], bank.ap, after=[tok])))
    project_tokens(k, w, 2560, 3072, x,
                   lambda t, bank, tok: bank.free(k.act_fn(gate[:, t, :], bank.ap, ACT.Silu, after=[tok])))
    k.barrier()

    k.arena.at = top
    o = k.arena(NT, HALF)
    sT = k.arena(2, 4, S)
    o_read = [None, None]
    decay = k.weights(d["decay"])
    for head in range(8):
        b = head % 2
        for kt in range(NT):
            n = S - kt * P
            bank = k.banks.take()
            t = k.mm(bank.ap[:, 0:n], kT[:, head, kt * P:(kt + 1) * P], qT[:, head // 2, kt * P:S], after=bank.wait)
            m_ = k.tt(sT[:, b, kt, 0:n], bank.ap[:, 0:n], decay.ap[:, head, 0:n], ALU.mult,
                      after=[t, decay.landed, o_read[b]])
            bank.free(m_)
        bank = k.banks.take()
        for t in range(NT):
            for kt in range(t + 1):
                tok = k.mm(bank.ap[:, t * DH:(t + 1) * DH], sT[:, b, kt, (t - kt) * P:(t - kt + 1) * P],
                           v[:, kt, head * DH:(head + 1) * DH], kt == 0, kt == t,
                           after=[m_, *bank.wait] if t == kt == 0 else ())
        o_read[b] = tok
        e = k.act_fn(o[:, :, head * DH:(head + 1) * DH], bank.ap[:, 0:NT * DH].rearrange("p (t d) -> p t d", d=DH),
                     ACT.Copy, after=[tok])
        bank.free(e)
    decay.done(m_)
    mu, var, sq = k.arena(NT, 8), k.arena(NT, 8), k.arena(HALF)
    assert k.arena.at <= keep
    for t in range(NT):
        x = o[:, t, :].rearrange("p (h d) -> p h d", d=DH)
        k.dve(nc.vector.tensor_reduce, mu[:, t, :], x, AX, ALU.add, after=[e])
        k.ts(mu[:, t, :], mu[:, t, :], 1.0 / DH, None, ALU.mult)
        k.tt(x, x, mu[:, t, :].unsqueeze(2).to_broadcast([P, 8, DH]), ALU.subtract)
        k.tt(sq, o[:, t, :], o[:, t, :], ALU.mult)
        k.dve(nc.vector.tensor_reduce, var[:, t, :], sq.rearrange("p (h d) -> p h d", d=DH), AX, ALU.add)
    inverse_root(k, var, var, 1.0 / DH)
    for t in range(NT):
        x = o[:, t, :].rearrange("p (h d) -> p h d", d=DH)
        k.tt(x, x, var[:, t, :].unsqueeze(2).to_broadcast([P, 8, DH]), ALU.mult)
        last = k.tt(o[:, t, :], o[:, t, :], gate[:, t, :], ALU.mult)
    for j in range(4):
        bank = k.banks.take()
        for t in range(NT):
            tok = k.tr(bank.ap[:, t * P:(t + 1) * P], o[:, t, j * P:(j + 1) * P], after=[last, *bank.wait])
        e = k.evac(catT[:, 4 + j, :], bank.ap, after=[tok])
        bank.free(e)
    k.barrier()
    k.arena.at = top
    return catT



def sparse_attention(k):
    d, nc = k.dram, k.nc
    oT = k.arena(NC, S)
    top = k.arena.at
    qT = k.arena(NC, S)
    ksT, kwT = k.arena(2, 2, S), k.arena(2, 2, S)
    vs, vw = k.arena(NT, 256), k.arena(NT, 256)
    kcT, vc = k.arena(2, 2, N_CMP), k.arena(256)
    gates = k.arena(NT, 48)
    hide, seen = k.arena(NT, N_CMP), k.arena(NT, N_CMP)
    causal = k.arena(P)
    keep = k.arena.at
    x = k.arena.parts(NC, S)
    ready = normed(k, d["attn_norm_2_cols"][1], x)
    cos, sin, ccos, csin = k.arena(NT, 8), k.arena(NT, 8), k.arena(8), k.arena(8)
    kc_in, vc_in = [x.rearrange("p t n -> p (t n)").rearrange("p (g s) -> p g s", g=2) for x in (vs, vw)]
    w1 = [oT[:, 4 * i:4 * i + 4, :].rearrange("p a b -> p (a b)").rearrange("p (l e) -> p l e", e=DH) for i in range(2)]
    w2, pe = [k.arena(DH) for _ in range(2)], [k.arena(32) for _ in range(2)]
    names = ("k", "v")
    pairs = [(cos, d["nsa_cos"]), (sin, d["nsa_sin"]), (ccos[0:N_CMP, :], d["cmp_cos"]), (csin[0:N_CMP, :], d["cmp_sin"]),
             (hide, d["cmp_hide"]), (seen, d["cmp_seen"]), (causal, d["causal"])]
    for i, n in enumerate(names):
        for p in range(2):
            q = slice(64 * p, 64 * p + 64)
            pairs += [(w1[i][q], d[f"cmp_{n}_w1_2"].rearrange("(l d) e -> d l e", d=DH)),
                      (w2[i][q], d[f"cmp_{n}_w2_2"]), (pe[i][q], d[f"cmp_pe_{n}_2_T"])]
    small = k.loads(pairs)
    for dst in (ksT, kwT, kcT):
        for i in range(2):
            k.dve(nc.vector.memset, dst[64 * (1 - i):64 * (1 - i) + 64, :, i, :], 0.0)
    w = d["nsa_w_in_2"]
    tm, half = k.arena(2, HALF), k.arena(2, 64)
    read = [None, None]
    turn = [0]

    def rotated(bank, tok, t, c0, c1, scale):
        b = turn[0] % 2
        turn[0] += 1
        n = (c1 - c0) // DH
        dst = tm[:, b, 0:c1 - c0]
        to, frm = dst, bank.ap[:, c0:c1]
        if n == 8:
            to = dst.rearrange("p (r g d) -> p g r d", g=2, r=4)
            frm = frm.rearrange("p (g r d) -> p g r d", g=2, r=4)
        a = k.act_fn(to, frm, ACT.Copy, scale=scale, after=[tok, read[b]])
        o = dst.rearrange("p (h d) -> p h d", d=DH)
        last = rotate(k, o[:, :, 0:8], o[:, :, 8:16], o[:, :, 0:8], o[:, :, 8:16], cos[:, t, :], sin[:, t, :],
                      [half[:, i, 0:8 * n] for i in range(2)], (P, n, 8), after=[a, small])
        return b, dst, a, last

    def use_q(a_):
        def use(t, bank, tok):
            b, dst, r, last = rotated(bank, tok, t, 0, HALF, DH ** -0.5)
            bank.free(r)
            out = k.banks.take()
            for g in range(4):
                tt = k.tr(out.ap[:, g * P:(g + 1) * P], dst[:, g * P:(g + 1) * P], after=[last, *out.wait])
            read[b] = tt
            e = k.evac(qT[:, 4 * a_:4 * a_ + 4, t * P:(t + 1) * P], out.ap.rearrange("p (g q) -> p g q", g=4), after=[tt])
            out.free(e)
        return use

    def use_kv(kdst, vdst):
        def use(t, bank, tok):
            b, dst, r, last = rotated(bank, tok, t, 0, 256, 1.0)
            r2 = k.act_fn(vdst[:, t, :], bank.ap[:, 256:512], ACT.Copy, after=[tok])
            bank.free(r2)
            out = k.banks.take()
            for g in range(2):
                tt = k.tr(out.ap[:, g * P:(g + 1) * P], dst[:, g * P:(g + 1) * P], after=[last, *out.wait])
            read[b] = tt
            for i in range(2):
                q = slice(64 * i, 64 * i + 64)
                e = k.dve(nc.vector.tensor_copy, kdst[q, :, i, t * P:(t + 1) * P],
                          out.ap[q, 0:2 * P].rearrange("p (g q) -> p g q", g=2), after=[tt])
            out.free(e)
        return use

    project_tokens(k, w, 0, 512, x, use_q(0), ready=[ready])
    project_tokens(k, w, 512, 1024, x, use_q(1))
    cmp_in = [kc_in[:, 0, :], kc_in[:, 1, :], vc_in[:, 0, :], vc_in[:, 1, :]]
    in_ready = []

    def use_cmp(j, bank, tok):
        e = k.evac(cmp_in[j], bank.ap, after=[tok])
        bank.free(e)
        in_ready.append(e)

    project_features(k, w, 1024, 1536, x, use_cmp)
    g_sb, bias = k.arena(2, 64), k.arena(2)
    cmp_tm = k.arena(256)
    for i, src in enumerate((kc_in, vc_in)):
        pe_bank = k.banks.take()
        for p in range(2):
            q = slice(64 * p, 64 * p + 64)
            for l in range(32):
                t = k.mm(pe_bank.ap[q, 0:1], w1[i][q, l, :], pe[i][q, l:l + 1], l == 0, l == 31,
                         after=[small, *pe_bank.wait] if l == 0 else ())
        v0 = k.dve(nc.vector.tensor_copy, bias[:, i:i + 1], pe_bank.ap[:, 0:1], after=[t])
        pe_bank.free(v0)
        bank = k.banks.take()
        for p in range(2):
            q = slice(64 * p, 64 * p + 64)
            for l in range(32):
                tokens = src[q, :, l:l + 16 * (N_CMP - 1) + 1:16]
                t = k.mm(bank.ap[q, 0:2 * N_CMP], w1[i][q, l, :], tokens, l == 0, l == 31,
                         after=[*in_ready, *bank.wait] if l == 0 else ())
        a = k.act_fn(g_sb[:, i, 0:2 * N_CMP], bank.ap[:, 0:2 * N_CMP], ACT.Gelu_apprx_tanh, bias=bias[:, i:i + 1], after=[t, v0])
        bank.free(a)
        dst = cmp_tm if i == 0 else vc
        for p in range(2):
            q = slice(64 * p, 64 * p + 64)
            bank2 = k.banks.take()
            for gp in range(2):
                t = k.mm(bank2.ap[0:N_CMP, gp * DH:(gp + 1) * DH], g_sb[q, i, gp * N_CMP:(gp + 1) * N_CMP], w2[i][q, :],
                         after=[a, *bank2.wait])
            c = k.dve(nc.vector.tensor_copy,
                      dst[0:N_CMP, :].rearrange("p (gp two d) -> p two gp d", two=2, d=DH)[:, p],
                      bank2.ap[0:N_CMP, 0:2 * DH].rearrange("p (gp d) -> p gp d", d=DH), after=[t])
            bank2.free(c)
        if i == 0:
            o = cmp_tm[0:N_CMP, :].rearrange("p (h d) -> p h d", d=DH)
            last = rotate(k, o[:, :, 0:8], o[:, :, 8:16], o[:, :, 0:8], o[:, :, 8:16], ccos[0:N_CMP, :], csin[0:N_CMP, :],
                          [half[0:N_CMP, j, 0:32] for j in range(2)], (N_CMP, 4, 8))
            out = k.banks.take()
            for gp in range(2):
                t = k.tr(out.ap[:, gp * N_CMP:(gp + 1) * N_CMP], cmp_tm[0:N_CMP, gp * P:(gp + 1) * P], after=[last, *out.wait])
            for j in range(2):
                q = slice(64 * j, 64 * j + 64)
                e = k.dve(nc.vector.tensor_copy, kcT[q, :, j, :],
                          out.ap[q, 0:2 * N_CMP].rearrange("p (g n) -> p g n", g=2), after=[t])
            out.free(e)

    project_tokens(k, w, 1536, 2048, x, use_kv(ksT, vs))
    project_tokens(k, w, 2048, 2560, x, use_kv(kwT, vw))
    project_tokens(k, w, 2560, 2608, x,
                   lambda t, bank, tok: bank.free(k.act_fn(gates[:, t, :], bank.ap[:, 0:48], ACT.Sigmoid, after=[tok])))
    k.barrier()
    k.arena.at = keep

    prob, stats = k.arena.place(k.unit_region, (2, 4, S)), k.arena(2, 3, 4)
    PT = [[k.arena(4, P if branch == 0 else S) for branch in range(3)] for _ in range(2)]
    keys, vals = (kcT, ksT, kwT), (vc, vs, vw)
    prob_read, pt_read = [None, None], [None, None]
    g_of = [gates[:, t, :].rearrange("p (a g r b) -> p b a r g", a=2, g=2, b=3) for t in range(NT)]
    steps = [(a_, r0, t, branch) for a_ in range(2) for r0 in (0, 2) for t in range(NT) for branch in range(3)]

    def heads_of(a_, r0):
        return [8 * a_ + 4 * p + r0 + i for i in range(2) for p in range(2)]

    def width_of(n):
        return N_CMP if steps[n][3] == 0 else (steps[n][2] + 1) * P

    def scores(n):
        a_, r0, t, branch = steps[n]
        width, made = width_of(n), []
        heads = 4 if branch == 0 else 2
        for j0 in range(0, 4, heads):
            run = score_banks.take_run(2)
            if branch == 0:
                sc = run.ap[:, 0, 0:4 * N_CMP].rearrange("p (h n) -> p h n", h=4)
            else:
                sc = run.ap[:, :, 0:width]
            for j in range(j0, j0 + heads):
                tok = k.mm(sc[:, j - j0, :], qT[:, 4 * a_ + r0 + j // 2, t * P:(t + 1) * P],
                           keys[branch][:, a_, j % 2, 0:width], after=run.wait if j == j0 else ())
            made.append((slice(j0, j0 + heads), run, sc, tok))
        return made

    def exps(n, heads, run, sc, tok):
        t, branch = steps[n][2:]
        b, width, count = n % 2, width_of(n), heads.stop - heads.start
        if branch == 0:
            k.tt(sc, sc, hide[:, t, :].unsqueeze(1).to_broadcast([P, count, N_CMP]), ALU.add, after=[tok])
        else:
            diag = run.ap[:, :, width - P:width]
            k.tt(diag, diag, causal.unsqueeze(1).to_broadcast([P, count, P]), ALU.add, after=[tok])
        done = exponentials(k, sc, count, width, 1.0, prob[:, b, heads], stats[:, b, :, heads],
                            after=[tok], out_free=[prob_read[b]])
        run.free(done)
        return done

    def transposes(n, heads, last):
        t, branch = steps[n][2:]
        b, tb = n % 2, (n // 3) % 2
        if branch == 0:
            out = k.banks.take()
            for j in heads:
                tok = k.tr(out.ap[0:N_CMP, j * P:(j + 1) * P], prob[:, b, j, 0:N_CMP], after=[last, *out.wait])
            e = k.evac(PT[tb][0][0:N_CMP], out.ap[0:N_CMP, :].rearrange("p (j q) -> p j q", j=4), after=[tok, pt_read[tb]])
            out.free(e)
        else:
            for j in heads:
                out = k.banks.take()
                for kt in range(t + 1):
                    tok = k.tr(out.ap[:, kt * P:(kt + 1) * P], prob[:, b, j, kt * P:(kt + 1) * P],
                               after=[last, *out.wait])
                e = k.evac(PT[tb][branch][:, j, 0:(t + 1) * P], out.ap[:, 0:(t + 1) * P], after=[tok, pt_read[tb]])
                out.free(e)
        prob_read[b] = tok

    def values(n, ready):
        a_, r0, t, _ = steps[n]
        tb = (n // 3) % 2
        out = k.banks.take()
        first = [*ready, *out.wait]
        for p in range(2):
            gc = slice((2 * a_ + p) * DH, (2 * a_ + p + 1) * DH)
            parts = [(vc[0:N_CMP, gc], PT[tb][0][0:N_CMP], slice(0, P))]
            parts += [(vals[branch][:, kt, gc], PT[tb][branch], slice(kt * P, (kt + 1) * P))
                      for branch in (1, 2) for kt in range(t + 1)]
            for m, (v_, pt, ks) in enumerate(parts):
                for i in range(2):
                    tok = k.mm(out.ap[64 * i:64 * i + 64, p * P:(p + 1) * P], v_, pt[:, 2 * i + p, ks],
                               m == 0, m == len(parts) - 1, after=first)
                    first = ()
        pt_read[tb] = tok
        return lambda: values_out(a_, r0, t, out, tok)

    def values_out(a_, r0, t, out, tok):
        c0 = 4 * a_ + r0 // 2
        e = k.evac(oT[:, c0:c0 + 3:2, t * P:(t + 1) * P], out.ap[:, 0:2 * P].rearrange("p (c q) -> p c q", c=2), after=[tok])
        out.free(e)

    all_banks = k.banks
    score_banks, k.banks = all_banks.part(0, 6), all_banks.part(6, 8)
    done, due = None, None
    for n in range(len(steps) + 1):
        made = scores(n) if n < len(steps) else []
        evacuate = values(*due) if due else lambda: None
        due = None
        if n:
            t, branch = steps[n - 1][2:]
            last = normalise(k, 4, width_of(n - 1), prob[:, (n - 1) % 2], stats[:, (n - 1) % 2], done,
                             gate=g_of[t][:, branch, steps[n - 1][0], steps[n - 1][1]:steps[n - 1][1] + 2, :],
                             keep=seen[:, t, :] if branch == 0 else None)
            groups = [range(4)] if branch == 0 else [range(2), range(2, 4)]
        else:
            groups = []
        for half in made:
            done = exps(n, *half)
        for group in groups:
            transposes(n - 1, group, last)
        evacuate()
        if n and n % 3 == 0:
            due = (n - 1, [k.dve.last, k.act.last])
    values(*due)()
    k.banks = all_banks
    k.barrier()
    k.arena.at = top
    return oT


def finish(k):
    nc = k.nc
    for line in (k.pe, k.dve, k.act, k.pool, k.sync):
        line.number()
    with nc.Block() as block:
        @block.sync
        def _(eng):
            k.sync.emit(eng)
            eng.wait_ge(k.out_count[0], k.out_count[1])

        @block.tensor
        def _(eng):
            k.pe.emit(eng)

        @block.vector
        def _(eng):
            k.dve.emit(eng)

        @block.scalar
        def _(eng):
            k.act.emit(eng)

        @block.gpsimd
        def _(eng):
            k.pool.emit(eng)



def build(nc, dram, out):
    with ExitStack() as ctx:
        k = Core(nc, ctx, dram)
        d = dram
        first = k.loads([(k.ident, d["ident"]), (k.slot_ids, d["slot_ids"]),
                 (k.sum_cols, d["sum_cols"])])
        h_landed = k.loads([(k.h[:, :, :], d["x"][0].rearrange("(t p) n -> p t n", p=P))])

        k.startup = [first, h_landed, k.dve(nc.vector.memset, k.ones, 1.0)]
        mods = [dict(cols=k.arena(48, 2)) for _ in range(2)]
        base = k.arena.at
        mods[0]["catT"] = k.arena(NC, S)
        mods[0]["raw_ctx"] = k.arena(NC, CTX)
        mods[0]["raw_landed"] = k.loads([(mods[0]["catT"], d["xT"].rearrange("(c p) s -> p c s", p=P)),
                                         (mods[0]["raw_ctx"], d["ctxT"].rearrange("(c p) s -> p c s", p=P))])
        after_cat = base + NC * S
        k.arena.at = k.arena.words // 8 * 8 - 2 * HALF - 48 - NC * 32 - 2 * NC
        scratch = dict(part=k.arena(2, HALF), bias_cols=k.arena(48), cond=k.arena(NC, 32))
        raw = k.arena(2, NC)
        for m in mods:
            m.update(scratch)
        small = k.loads([(raw[:, 0, :], d["c_cols"][0]), (raw[:, 1, :], d["c_ctx_cols"])])
        z = k.dve(nc.vector.memset, scratch["cond"], 0.0)
        for i in range(2):
            k.cond_ready = k.act_fn(scratch["cond"][:, :, i], raw[:, i, :], ACT.Silu, after=[z, small, *k.startup])
        for _ in modulation_steps(k, 0, mods[0]):
            pass
        k.barrier()
        k.arena.at = after_cat
        for layer, m in enumerate(mods):
            w_out = d["w_mix_out"] if layer == 0 else d["w_conv_out"]
            mixT = attn_pool(k, m, modulation_steps(k, 1, mods[1])) if layer == 0 else short_conv(k, m)
            gain, bias = k.arena(D), k.arena(D)
            ready = k.loads([(gain, d["ln_mix_g"][layer, :].partition_broadcast(P)),
                             (bias, d["ln_mix_b"][layer, :].partition_broadcast(P))])
            gate, spread_done = spread(k, m["cols"][:, 16:24, 0])
            use = post_norm(k, gate, gain, bias, spread_done, [ready])
            project_out(k, w_out, lambda c: mixT[:, c, :], use)
            k.barrier()
            k.arena.at = base
            slotsT, ye = experts(k, layer, m)
            gain, bias = k.arena(D), k.arena(D)
            ready = k.loads([(gain, d["ln_ffn_g"][layer, :].partition_broadcast(P)),
                             (bias, d["ln_ffn_b"][layer, :].partition_broadcast(P))])
            gate, spread_done = spread(k, m["cols"][:, 40:48, 0])
            use = post_norm(k, gate, gain, bias, spread_done, [ready])
            scatter(k, slotsT, ye, use)
            k.barrier()
            k.arena.at = base

        k.arena.at = 0
        catT = recurrent_retention(k)
        project_out(k, d["ab_w_out_2"], lambda c: catT[:, c, :], add_residual(k))
        k.barrier()
        k.arena.at = 0
        swiglu(k, 0)
        oT = sparse_attention(k)
        project_out(k, d["nsa_w_out_2"], lambda c: oT[:, c, :], add_residual(k))
        k.barrier()
        k.arena.at = 0
        swiglu(k, 1)

        scaled, r, gain = k.arena(NT, D), k.arena(NT), k.arena(D)
        small = k.loads([(gain, d["final_norm_2"].partition_broadcast(P))])
        rms_scaled(k, scaled, r)
        for t in range(NT):
            last = k.tt(scaled[:, t, :], scaled[:, t, :], gain, ALU.mult, after=[small])
            stored = k.sync.dma(nc.sync.dma_start, out[0, t * P:(t + 1) * P, :], scaled[:, t, :], k.out_count, after=[last])

        finish(k)



def feature_columns(v):
    return np.swapaxes(v.reshape(*v.shape[:-1], -1, P), -1, -2)


def kernel(**inputs):
    import concourse.bacc as bacc
    from concourse.bass_utils import run_bass_kernel_spmd

    a = {n: np.asarray(v) for n, v in inputs.items()}
    a["xT"] = np.ascontiguousarray(a["x"][0].T)
    a["ctxT"] = np.ascontiguousarray(a.pop("ctx")[0].T)
    for name in ("w_mix_in", "q_norm_g", "k_norm_g", "w_pool_grp", "pool_scale", "w_mix_out", "w_conv_in", "conv_w",
                 "w_conv_out", "ab_w_in_2", "conv_w_2", "conv_b_2", "gate_a_w_2", "gate_a_b_2", "gate_x_w_2",
                 "gate_x_b_2", "lru_lambda_2", "ab_w_out_2", "nsa_w_in_2", "cmp_pe_k_2", "cmp_k_w1_2", "cmp_k_w2_2",
                 "cmp_pe_v_2", "cmp_v_w1_2", "cmp_v_w2_2", "nsa_w_out_2"):
        a[name] = a[name][0]
    for name in ("c", "c_ctx", "b_mod", "pool_scale", "attn_norm_2", "ffn_norm_2", "conv_b_2", "gate_a_b_2",
                 "gate_x_b_2", "lru_lambda_2"):
        a[name + "_cols"] = feature_columns(a[name])
    for name in ("conv_w", "conv_w_2"):
        a[name + "_cols"] = feature_columns(a.pop(name)).transpose(1, 0, 2)
    for name in ("cmp_pe_k_2", "cmp_pe_v_2"):
        a[name + "_T"] = a.pop(name).T
    for name in ("c", "c_ctx", "pool_scale", "attn_norm_2", "ffn_norm_2", "conv_b_2", "gate_a_b_2", "gate_x_b_2",
                 "lru_lambda_2"):
        a.pop(name)
    a.update(shape_constants())
    nc = bacc.Bacc("TRN2", target_bir_lowering=False, num_devices=1)
    arrays, dram = {}, {}
    for name, v in a.items():
        v = np.ascontiguousarray(v)
        arrays[f"in_{name}"] = v
        dram[name] = nc.dram_tensor(f"in_{name}", v.shape, F32, kind="ExternalInput").ap()
    out = nc.dram_tensor("out", (1, S, D), F32, kind="ExternalOutput").ap()
    build(nc, dram, out)
    r = run_bass_kernel_spmd(nc, [arrays], core_ids=[0])
    return r.results[0]["out"]
```
